# Optimizing a Trainium2 kernel written in Bass

```python
import math
import jax, jax.numpy as jnp
from jax import lax
import numpy as np

D_MODEL = 1024
BATCH = 1
SEQ = 512
DEPTH = 2
DEC_BATCH = 8
DEC_SEQ = 1
PAST_LEN = 4096
PAGE_SIZE = 128

MIX_W = D_MODEL
W_A = MIX_W // 2
W_B = MIX_W - W_A
H_A = 8
HD_A = W_A // H_A
H_B = 8
HD_B = W_B // H_B
CHUNK = 128
CONV_W = 4
C_RG = 8.0
D_FF = 2816
PLE_DIM = 256
IN_W = 2 * W_A + 2 * W_B
EPS = 1e-6

kernel_name = "hymba_gmlp_rglru_macaron_decoder_step"

def rms_norm(x, g):
    xf = x.astype(jnp.float32)
    y = xf * lax.rsqrt(jnp.mean(xf * xf, axis=-1, keepdims=True) + EPS)
    return (y * g.astype(jnp.float32)).astype(x.dtype)

def layer_norm(x, g, b):
    xf = x.astype(jnp.float32)
    mu = jnp.mean(xf, axis=-1, keepdims=True)
    xc = xf - mu
    y = xc * lax.rsqrt(jnp.mean(xc * xc, axis=-1, keepdims=True) + EPS)
    return (y * g.astype(jnp.float32) + b.astype(jnp.float32)).astype(x.dtype)

def swiglu(x, wg, wu, wd):
    return (jax.nn.silu(x @ wg) * (x @ wu)) @ wd

def chunk_spatial_gate(v, w_s, b_s):
    B, L, _ = v.shape
    n = -(-L // CHUNK)
    vp = jnp.pad(v, ((0, 0), (0, n * CHUNK - L), (0, 0)))
    vc = vp.reshape(B, n, CHUNK, H_A, HD_A)
    mask = jnp.tril(jnp.ones((CHUNK, CHUNK), dtype=bool))
    w = jnp.where(mask[None], w_s, jnp.zeros_like(w_s))
    s = jnp.einsum('hij,bnjhd->bnihd', w, vc) + b_s.T[None, None, :, :, None]
    return s.reshape(B, n * CHUNK, W_A)[:, :L]

def causal_conv(x, buf, w, b):
    L = x.shape[1]
    xp = jnp.concatenate([buf.astype(x.dtype), x], axis=1)
    y = b
    for k in range(CONV_W):
        y = y + xp[:, k:k + L] * w[k]
    return y, xp[:, -(CONV_W - 1):]

def block_diag(x, w, b):
    B, L, _ = x.shape
    xh = x.reshape(B, L, H_B, HD_B)
    return jnp.einsum('blhi,hij->blhj', xh, w).reshape(B, L, W_B) + b

def rg_lru(x, h0, w_r, b_r, w_i, b_i, lam):
    xf = x.astype(jnp.float32)
    r = jax.nn.sigmoid(block_diag(xf, w_r.astype(jnp.float32), b_r.astype(jnp.float32)))
    i = jax.nn.sigmoid(block_diag(xf, w_i.astype(jnp.float32), b_i.astype(jnp.float32)))
    log_a = -C_RG * r * jax.nn.softplus(-lam.astype(jnp.float32))
    a = jnp.exp(log_a)
    u = jnp.sqrt(jnp.maximum(-jnp.expm1(2.0 * log_a), 0.0)) * (i * xf)

    def step(h, inp):
        a_t, u_t = inp
        h = a_t * h + u_t
        return h, h

    hT, hs = lax.scan(step, h0.astype(jnp.float32), (jnp.swapaxes(a, 0, 1), jnp.swapaxes(u, 0, 1)))
    return jnp.swapaxes(hs, 0, 1).astype(x.dtype), hT.astype(h0.dtype)

def hybrid_mix(h, buf, h0, w_in, ln_v_g, ln_v_b, w_s, b_s, conv_w, conv_b,
               w_r, b_r, w_i, b_i, lam, w_out):
    z = h @ w_in
    u = jax.nn.gelu(z[..., :W_A])
    v = layer_norm(jax.nn.gelu(z[..., W_A:2 * W_A]), ln_v_g, ln_v_b)
    xr = z[..., 2 * W_A:2 * W_A + W_B]
    gt = z[..., 2 * W_A + W_B:]
    y_a = u * chunk_spatial_gate(v, w_s, b_s)
    xc, new_buf = causal_conv(xr, buf, conv_w, conv_b)
    yr, hT = rg_lru(xc, h0, w_r, b_r, w_i, b_i, lam)
    y_b = yr * jax.nn.gelu(gt)
    out = jnp.concatenate([y_a, y_b], axis=-1) @ w_out
    return out, v, new_buf, hT

def setup_inputs(seed: int = 0) -> dict:
    key = jax.random.key(seed)
    ks = iter(jax.random.split(key, 48))
    f32 = jnp.float32

    def nrm(shape, scale):
        return jax.random.normal(next(ks), shape, f32) * scale

    def gain(shape):
        return 1.0 + 0.05 * jax.random.normal(next(ks), shape, f32)

    x_prompt = nrm((BATCH, SEQ, D_MODEL), 1.0)
    x_sample = nrm((DEC_BATCH, DEC_SEQ, D_MODEL), 1.0)
    state_h = nrm((DEPTH, DEC_BATCH, W_B), 0.5)
    state_conv = nrm((DEPTH, DEC_BATCH, CONV_W - 1, W_B), 1.0)
    p_prompt = nrm((DEPTH, BATCH, SEQ, PLE_DIM), 1.0)
    p_sample = nrm((DEPTH, DEC_BATCH, DEC_SEQ, PLE_DIM), 1.0)

    u_a = jax.random.uniform(next(ks), (DEPTH, W_B), f32, minval=0.9, maxval=0.999)
    a0 = u_a ** (1.0 / C_RG)
    lam = jnp.log(a0) - jnp.log1p(-a0)

    return {
        "x_prompt": x_prompt, "x_sample": x_sample,
        "state_h": state_h, "state_conv": state_conv,
        "p_prompt": p_prompt, "p_sample": p_sample,
        "n_ffn1": gain((DEPTH, D_MODEL)),
        "w_ffn1_gate": nrm((DEPTH, D_MODEL, D_FF), D_MODEL ** -0.5),
        "w_ffn1_up": nrm((DEPTH, D_MODEL, D_FF), D_MODEL ** -0.5),
        "w_ffn1_down": nrm((DEPTH, D_FF, D_MODEL), D_FF ** -0.5),
        "n_mix": gain((DEPTH, D_MODEL)),
        "w_in": nrm((DEPTH, D_MODEL, IN_W), D_MODEL ** -0.5),
        "ln_v_g": gain((DEPTH, W_A)),
        "ln_v_b": nrm((DEPTH, W_A), 0.02),
        "w_s": nrm((DEPTH, H_A, CHUNK, CHUNK), CHUNK ** -0.5),
        "b_s": gain((DEPTH, H_A, CHUNK)),
        "conv_w": nrm((DEPTH, CONV_W, W_B), CONV_W ** -0.5),
        "conv_b": nrm((DEPTH, W_B), 0.02),
        "w_r": nrm((DEPTH, H_B, HD_B, HD_B), HD_B ** -0.5),
        "b_r": nrm((DEPTH, W_B), 0.02),
        "w_i": nrm((DEPTH, H_B, HD_B, HD_B), HD_B ** -0.5),
        "b_i": nrm((DEPTH, W_B), 0.02),
        "lam": lam,
        "w_out": nrm((DEPTH, MIX_W, D_MODEL), MIX_W ** -0.5),
        "n_ffn2": gain((DEPTH, D_MODEL)),
        "w_ffn2_gate": nrm((DEPTH, D_MODEL, D_FF), D_MODEL ** -0.5),
        "w_ffn2_up": nrm((DEPTH, D_MODEL, D_FF), D_MODEL ** -0.5),
        "w_ffn2_down": nrm((DEPTH, D_FF, D_MODEL), D_FF ** -0.5),
        "n_ple": gain((DEPTH, D_MODEL)),
        "w_ple_gate": nrm((DEPTH, D_MODEL, D_MODEL), D_MODEL ** -0.5),
        "w_ple_proj": nrm((DEPTH, PLE_DIM, D_MODEL), PLE_DIM ** -0.5),
        "n_final": gain((D_MODEL,)),
    }

def reference(x_prompt, x_sample, state_h, state_conv, p_prompt, p_sample,
              n_ffn1, w_ffn1_gate, w_ffn1_up, w_ffn1_down,
              n_mix, w_in, ln_v_g, ln_v_b, w_s, b_s, conv_w, conv_b,
              w_r, b_r, w_i, b_i, lam, w_out,
              n_ffn2, w_ffn2_gate, w_ffn2_up, w_ffn2_down,
              n_ple, w_ple_gate, w_ple_proj, n_final):
    B = x_prompt.shape[0]
    xp, xs = x_prompt, x_sample
    buf_p0 = jnp.zeros((B, CONV_W - 1, W_B), x_prompt.dtype)
    h_p0 = jnp.zeros((B, W_B), state_h.dtype)
    hp_out, cp_out, hs_out, cs_out, vs_out = [], [], [], [], []

    for i in range(DEPTH):
        def layer(x, p, buf, h0):
            x = x + 0.5 * swiglu(rms_norm(x, n_ffn1[i]), w_ffn1_gate[i], w_ffn1_up[i], w_ffn1_down[i])
            mix, v, new_buf, hT = hybrid_mix(
                rms_norm(x, n_mix[i]), buf, h0, w_in[i], ln_v_g[i], ln_v_b[i], w_s[i], b_s[i],
                conv_w[i], conv_b[i], w_r[i], b_r[i], w_i[i], b_i[i], lam[i], w_out[i])
            x = x + mix
            x = x + 0.5 * swiglu(rms_norm(x, n_ffn2[i]), w_ffn2_gate[i], w_ffn2_up[i], w_ffn2_down[i])
            gate = jax.nn.sigmoid(rms_norm(x, n_ple[i]) @ w_ple_gate[i])
            x = x + gate * (p @ w_ple_proj[i])
            return x, v, new_buf, hT

        xp, _, cbuf_p, hT_p = layer(xp, p_prompt[i], buf_p0, h_p0)
        xs, v_s, cbuf_s, hT_s = layer(xs, p_sample[i], state_conv[i], state_h[i])
        hp_out.append(hT_p)
        cp_out.append(cbuf_p)
        hs_out.append(hT_s)
        cs_out.append(cbuf_s)
        vs_out.append(v_s)

    y_prompt = rms_norm(xp, n_final)
    y_sample = rms_norm(xs, n_final)
    state_h_prompt = jnp.stack(hp_out)
    state_conv_prompt = jnp.stack(cp_out)
    state_h_sample = jnp.stack(hs_out)
    state_conv_sample = jnp.stack(cs_out)
    chunk_v_sample = jnp.stack(vs_out)
    return (y_prompt, y_sample, state_h_prompt, state_conv_prompt, state_h_sample, state_conv_sample, chunk_v_sample)


_drawn_inputs = setup_inputs


def setup_inputs(seed=0):
    import zlib

    import numpy as np

    out = dict(_drawn_inputs(seed))
    spreads = {}
    factors = {'ln_v_b': 2.88, 'b_r': 8.0, 'b_i': 7.075, 'n_ffn2': 2.68, 'n_ple': 19.723}
    for name, (base, spread) in spreads.items():
        noise = np.random.default_rng([zlib.crc32(name.encode()), seed]).standard_normal(out[name].shape)
        drawn = base * np.exp(spread * noise) if base else spread * noise
        out[name] = __import__('jax').numpy.asarray(drawn.astype(out[name].dtype))
    for name, factor in factors.items():
        out[name] = (out[name] * factor).astype(out[name].dtype)
    return out
```

```python
from contextlib import ExitStack

import concourse.bass as bass
from concourse import mybir

F32 = mybir.dt.float32
F32R = mybir.dt.float32r
ALU = mybir.AluOpType
ACT = mybir.ActivationFunctionType

P = 128
DEPTH, SEQ, NSAMP, DM, DFF, PLE = 2, 512, 8, 1024, 2816, 256
WA = WB = 512
CONV = 4
CHUNK = 128
HD = 64
TOK = SEQ + NSAMP
HALF = TOK // 2
XT = DM // P
MT = WA // P
NCH = SEQ // CHUNK
EPS = 1e-6
LRU_C = 8.0
FFN_CHUNKS = (8, 8, 6)
assert sum(FFN_CHUNKS) * P == DFF
SLOTS = 4
UNIT = 8 * P
AHEAD = 3

FFN_UNITS = sum(2 * t + XT for t in FFN_CHUNKS)
U_F1 = 0
U_XR = U_F1 + FFN_UNITS
U_V = U_XR + MT
U_GT = U_V + MT
U_U = U_GT + MT
U_OUT = U_U + MT
U_F2 = U_OUT + XT
U_PP = U_F2 + FFN_UNITS
U_PG = U_PP + XT // 2
UNITS = U_PG + XT
TOTAL = DEPTH * UNITS

G_F1 = 0
G_XR = G_F1 + FFN_UNITS
G_GT = G_XR + MT
G_U = G_GT + MT
G_OUT = G_U + MT
G_F2 = G_OUT + XT
G_PP = G_F2 + FFN_UNITS
G_PG = G_PP + XT // 2
GROUPS = G_PG + XT

HT0 = sum(FFN_CHUNKS)
HT = 2 * HT0 + XT
FS_MIX = 2 * MT
FS = 2 * HT0 + FS_MIX + XT

V_G = 0
V_GF = V_G + DEPTH * 4 * XT
V_LAM = V_GF + XT
V_BR = V_LAM + DEPTH * MT
V_BI = V_BR + DEPTH * MT
V_CW = V_BI + DEPTH * MT
V_CB = V_CW + DEPTH * MT * CONV
V_W00 = V_CB + DEPTH * MT
V_B00 = V_W00 + DEPTH * MT
NV = V_B00 + DEPTH * MT

S_H, S_C, S_HS, S_CS = 0, 1, 4, 4 + NSAMP
NS = S_CS + 3 * NSAMP


def main_slot(g):
    layer, k = divmod(g, GROUPS)
    return (g + layer + (k >= G_GT)) % 2


def trunk(nc, weights, x_in, p_in, vecs_in, ln_in, bs_in, ws_in, bd_in, sc_in, sh_in,
          y_out, st_out, v_out):
    ctx = ExitStack()
    with ctx:
        def sb(name, shape, dt=F32):
            return ctx.enter_context(nc.sbuf_tensor(name, shape, dt))

        def sem(name):
            return ctx.enter_context(nc.semaphore(name))

        x = sb("x", [P, XT, TOK])
        xg_hi = sb("xg_hi", [P, XT, TOK], F32R)
        xg_lo = sb("xg_lo", [P, XT, TOK], F32R)
        raw = sb("raw", [P, SLOTS, UNIT])
        w_hi = sb("w_hi", [P, SLOTS, UNIT], F32R)
        w_lo = sb("w_lo", [P, SLOTS, UNIT], F32R)
        h_hi = sb("h_hi", [P, XT, TOK], F32R)
        h_lo = sb("h_lo", [P, XT, TOK], F32R)
        pe_hi = sb("pe_hi", [P, 2, TOK], F32R)
        pe_lo = sb("pe_lo", [P, 2, TOK], F32R)
        rstd_b = sb("rstd_b", [P, TOK])
        tmp = sb("tmp", [P, 6, TOK])
        mix = sb("mix", [P, 2 * MT * TOK + 2 * (TOK + CONV - 1) + (NCH + 1) * WA])
        vecs = sb("vecs", [P, NV])
        ln = sb("ln", [P, 2, WA])
        bs = sb("bs", [P, MT, CHUNK])
        ws = sb("ws", [P, 2 * MT, CHUNK])
        bd = sb("bd", [P, 2, MT, P])
        sconv = sb("sconv", [P, MT, 3, NSAMP])
        sh0 = sb("sh0", [P, MT, NSAMP])
        states = sb("states", [P, DEPTH, MT, NS])
        ident = sb("ident", [P, P])
        ones = sb("ones", [P, P])
        small = sb("small", [P, 64])
        lam8 = sb("lam8", [P, 2, DEPTH * MT])
        lt = sb("lt", [P, 4, DEPTH * MT])

        def region(at, *dims):
            n = 1
            for d in dims:
                n *= d
            v = mix[:, at:at + n]
            return (v if len(dims) == 1 else v.rearrange("p (a b) -> p a b", a=dims[0])), at + n

        XRW = TOK + CONV - 1
        xc, at = region(0, MT, TOK)
        gt, at = region(at, MT, TOK)
        proj, _ = region(0, XT, TOK)
        xr, at = region(at, 2, XRW)
        praw, _ = region(at, 2, TOK)
        vt, at = region(at, NCH + 1, WA)
        diag = tmp[:, 4:6, :].rearrange("p a b -> p (a b)")[:, 0:(NCH + 1) * P]
        diag = diag.rearrange("p (a b) -> p a b", a=NCH + 1)
        rs = sb("rs", [P, 3, TOK])
        rs_sum = rs[:, 2, :]

        def sq(n):
            return rs[:, n % 2, :]

        VN = 2 * (NCH + 1) + 1 + (NCH + 1)

        def vn_tile(t):
            return 2 * (NCH + 1) + 1 + t + 1

        LV_CONV, LV_TILE = 2 * CONV, 8
        LV = MT * (LV_CONV + LV_TILE)
        LAM_STEPS = 25
        eps = small[:, 0:1]
        std = small[:, 8:13]
        rstd_t = small[:, 16:21]
        mv = small[:, 24:34].rearrange("p (a b) -> p a b", a=5)
        vstd = small[:, 34:39]
        vrstd = small[:, 40:45]
        bst = sb("bst", [P, 5, 6])

        main = [ctx.enter_context(nc.psum_tensor(f"main{i}", [P, 2, 512], F32)) for i in range(2)]
        aux = [ctx.enter_context(nc.psum_tensor(f"aux{i}", [P, 2, 512], F32)) for i in range(2)]
        vbank = [aux[0][:, 0, :], aux[0][:, 1, :], aux[1][:, 0, :], aux[1][:, 1, :]]

        raw_in = [sem(f"raw_in{s}") for s in range(SLOTS)]
        whi = sem("whi")
        wlo = sem("wlo")
        unit = sem("unit")
        evac = sem("evac")
        x_in_s = sem("x_in_s")
        v_st = sem("v_st")
        x_tmp = sem("x_tmp")
        vec_s = sem("vec_s")
        par_s = sem("par_s")
        p_s = sem("p_s")
        const_s = sem("const_s")
        mask_s = sem("mask_s")
        lamv = sem("lamv")
        lama = sem("lama")
        sq_s = sem("sq_s")
        ssum_s = sem("ssum_s")
        xhi = sem("xhi")
        xlo = sem("xlo")
        x_new = sem("x_new")
        st1 = sem("st1")
        std_s = sem("std_s")
        rt_s = sem("rt_s")
        dg_s = sem("dg_s")
        st2 = sem("st2")
        rb_s = sem("rb_s")
        f_s = sem("f_s")
        hf_s = sem("hf_s")
        hhi = sem("hhi")
        hlo = sem("hlo")
        ri = sem("ri")
        ri_ev = sem("ri_ev")
        la = sem("la")
        lv = sem("lv")
        v_ev = sem("v_ev")
        vn = sem("vn")
        va = sem("va")
        vp = sem("vp")
        sg = sem("sg")
        sg_ev = sem("sg_ev")
        p_v = sem("p_v")
        p_a = sem("p_a")
        pp_ev = sem("pp_ev")
        stc = sem("stc")
        pst = sem("pst")
        y_s = sem("y_s")
        out_s = sem("out_s")

        def pair(ps):
            return ps[:, :, 0:HALF]

        def halves(ap):
            return ap.rearrange("p (a b) -> p a b", a=2)

        def T(k):
            return tmp[:, k, :]

        def gain(stat, o):
            return vecs[:, V_G + stat * XT + o:V_G + stat * XT + o + 1]

        def vec(base, layer, m):
            c = base + layer * MT + m
            return vecs[:, c:c + 1]

        block = ctx.enter_context(nc.Block())

        @block.sync
        def _(sp):
            for n in range(SLOTS):
                sp.dma_start(raw[:, n, :], weights[n, :, :]).then_inc(raw_in[n], 16)
            with sp.Fori(1, TOTAL // SLOTS) as i:
                for s in range(SLOTS):
                    sp.wait_ge(wlo, i * SLOTS + (s - SLOTS + 1))
                    sp.dma_start(raw[:, s, :].rearrange("p (a n) -> p a n", a=1),
                                 weights[bass.ds(i * SLOTS + s, 1), :, :].rearrange("a p n -> p a n")
                                 ).then_inc(raw_in[s], 16)
            sp.wait_ge(stc, DEPTH * MT * 2)
            sp.wait_ge(pst, DEPTH * MT * 3)
            sp.dma_start(st_out, states[:, :, :, :].rearrange("p l m n -> p (l m n)")).then_inc(out_s, 16)
            for o in range(XT):
                sp.wait_ge(y_s, o + 1)
                sp.dma_start(y_out[:, o, :], x[:, o, :]).then_inc(out_s, 16)
            sp.wait_ge(out_s, 16 * (1 + XT))

        @block.gpsimd
        def _(pool):
            pool.memset(ident[:, :], 0.0).then_inc(const_s, 1)
            pool.memset(ones[:, :], 1.0).then_inc(const_s, 1)
            pool.memset(small[:, :], EPS).then_inc(const_s, 1)
            pool.memset(bd[:, :, :, :], 0.0).then_inc(const_s, 1)
            for b in range(2):
                pool.memset(xr[:, b, 0:CONV - 1], 0.0).then_inc(const_s, 1)
            pool.wait_ge(const_s, 6)
            pool.affine_select(out=ident[:, :], in_=ident[:, :], compare_op=ALU.not_equal, fill=1.0,
                               base=0, pattern=[[-1, P]], channel_multiplier=1).then_inc(const_s, 1)

            def load_layer(l):
                if l > 0:
                    pool.wait_ge(hlo, HT * l - HT + HT0 + XT)
                    pool.wait_ge(sg_ev, 2 * MT * l)
                    pool.wait_ge(stc, MT * 2 * l)
                    pool.wait_ge(pst, MT * 3 * l)
                pool.dma_start(ln[:, :, :], ln_in[l]).then_inc(par_s, 16)
                pool.dma_start(bs[:, :, :], bs_in[l]).then_inc(par_s, 16)
                pool.dma_start(ws[:, :, :], ws_in[l]).then_inc(par_s, 16)
                pool.dma_start(sconv[:, :, :, :].rearrange("p m k b -> p (m k b)"), sc_in[l]).then_inc(par_s, 16)
                pool.dma_start(sh0[:, :, :].rearrange("p m b -> p (m b)"), sh_in[l]).then_inc(par_s, 16)
                for q in range(2):
                    for j in range(2):
                        pool.dma_start(bd[HD * j:HD * j + HD, q, :, HD * j:HD * j + HD],
                                       bd_in[l, j, q]).then_inc(par_s, 16)
                pool.wait_ge(par_s, 9 * 16 * (l + 1))
                pool.affine_select(out=ws[:, :, :], in_=ws[:, :, :], compare_op=ALU.is_ge, fill=0.0,
                                   base=0, pattern=[[0, 2 * MT], [1, CHUNK]],
                                   channel_multiplier=-1).then_inc(mask_s, 1)

            def sums(stat):
                for o in range(XT):
                    n = stat * XT + o
                    pool.wait_ge(sq_s, n + 1)
                    if o == 0:
                        if stat:
                            pool.wait_ge(st1, stat)
                        pool.tensor_copy(rs_sum, sq(n)).then_inc(ssum_s, 1)
                    else:
                        pool.wait_ge(ssum_s, n)
                        pool.tensor_tensor(rs_sum, rs_sum, sq(n), ALU.add).then_inc(ssum_s, 1)

            def conv_states(l):
                for m in range(MT):
                    c = l * MT + m
                    pool.wait_ge(evac, l * GROUPS + G_XR + m + 1)
                    pool.tensor_copy(states[:, l, m, S_C:S_C + 3], xr[:, m % 2, SEQ:SEQ + 3]).then_inc(pst, 1)
                    pool.tensor_copy(states[:, l, m, S_CS:S_CS + 2 * NSAMP],
                                     sconv[:, m, 1:3, :].rearrange("p k b -> p (k b)")).then_inc(pst, 1)
                    pool.tensor_copy(states[:, l, m, S_CS + 2 * NSAMP:NS],
                                     xr[:, m % 2, SEQ + 3:SEQ + 3 + NSAMP]).then_inc(pst, 1)

            sums(0)
            load_layer(0)
            for l in range(DEPTH):
                sums(4 * l + 1)
                conv_states(l)
                for t in range(NCH + 1):
                    n = 2 * ((NCH + 1) * l + t)
                    pool.wait_ge(vn, VN * l + vn_tile(t))
                    pool.tensor_tensor(vt[:, t, :], vt[:, t, :], ln[:, 0, :], ALU.mult).then_inc(vp, 1)
                    pool.wait_ge(vp, n + 1)
                    pool.tensor_tensor(vt[:, t, :], vt[:, t, :], ln[:, 1, :], ALU.add).then_inc(vp, 1)
                pool.wait_ge(vp, 2 * (NCH + 1) * (l + 1))
                pool.dma_start(v_out[l, :, :], vt[P - NSAMP:P, NCH, :]).then_inc(v_st, 16)
                pool.wait_ge(v_st, 16 * (l + 1))
                pool.wait_ge(sg, MT * (l + 1))
                pool.dma_start(praw, p_in[l]).then_inc(p_s, 16)
                sums(4 * l + 2)
                if l + 1 < DEPTH:
                    load_layer(l + 1)
                sums(4 * l + 3)
                sums(4 * l + 4)

        @block.tensor
        def _(pe):
            def acc(ps, s, kts, hi, lo, order=None, k_wait=None, stop=None, mids=None, col0=0):
                order = order or range(kts)
                order = list(order)
                for a, k in enumerate(order):
                    if k_wait is not None:
                        k_wait(a)
                    w = slice(col0 + k * P, col0 + (k + 1) * P)
                    for b, (ww, xx) in enumerate(((w_hi, hi), (w_hi, lo), (w_lo, hi))):
                        for q in range(2):
                            last = pe.matmul(ps[:, q, 0:HALF], ww[:, s, w], xx[:, k, q * HALF:(q + 1) * HALF],
                                             start=(a == 0 and b == 0), stop=(a == kts - 1 and b == 2))
                    if mids and a in mids:
                        mids[a]()
                return last

            def weights_in(n):
                pe.wait_ge(wlo, n + 1)

            def free_main(G, first_after_v=0, layer=0):
                if first_after_v == 1:
                    pe.wait_ge(evac, G)
                elif first_after_v == 2:
                    pe.wait_ge(v_ev, (NCH + 1) * (layer + 1))
                else:
                    if not (isinstance(G, int) and G < 2):
                        pe.wait_ge(evac, G - 1)

            def stat1(stat):
                pe.wait_ge(ssum_s, XT * (stat + 1))
                for t in range(NCH + 1):
                    c = t * P if t < NCH else TOK - P
                    last = pe.matmul(aux[1][:, 0, t:t + 1], rs_sum[:, c:c + P], ones[:, 0:1], start=True, stop=True)
                last.then_inc(st1, 1)

            def stat2(stat):
                pe.wait_ge(dg_s, stat + 1)
                for t in range(NCH):
                    pe.matmul(aux[0][:, 0, t * P:(t + 1) * P], ones[:, :], diag[:, t, :], start=True, stop=True)
                pe.matmul(aux[0][:, 1, 0:NSAMP], ones[:, :], diag[:, NCH, P - NSAMP:P],
                          start=True, stop=True).then_inc(st2, 1)

            def ffn(l, which, u0, g0):
                stat = 4 * l + 2 * which
                n, G, h = l * UNITS + u0, l * GROUPS + g0, l * HT + which * (HT0 + XT)
                for c, tiles in enumerate(FFN_CHUNKS):
                    def up(n, G, par, first=False):
                        for j in range(2 * 2):
                            weights_in(n + j)
                            free_main(G + j)
                            kw, mids = None, None
                            if first and j == 0:
                                kw = lambda a: pe.wait_ge(xlo, XT * stat + a + 1)
                                mids = {5: lambda: stat1(stat)}
                            if first and j == 1:
                                mids = {2: lambda: stat2(stat)}
                            acc(main[(par + j) % 2], j, XT, xg_hi, xg_lo, k_wait=kw,
                                mids=mids).then_inc(unit, 1)
                    par = main_slot(G)
                    start = 0
                    if c == 0:
                        up(n, G, par, True)
                        start = 1
                    with pe.Fori(start, tiles // 2) as i:
                        up(i * 4 + n, i * 4 + G, par)
                    n, G, h = n + 2 * tiles, G + 2 * tiles, h + tiles
                    with pe.Fori(0, 2) as i:
                        for j in range(4):
                            weights_in(i * 4 + (n + j))
                            free_main(i * 4 + (G + j))
                            kw = None
                            if j == 0:
                                kw = lambda a: pe.wait_ge(hlo, h - tiles + a + 1)
                            acc(main[(par + j) % 2], j, tiles, h_hi, h_lo, k_wait=kw).then_inc(unit, 1)
                    n, G = n + XT, G + XT

            pe.wait_ge(const_s, 7)
            for l in range(DEPTH):
                N, G0 = l * UNITS, l * GROUPS
                ffn(l, 0, U_F1, G_F1)

                stat = 4 * l + 1
                for m in range(MT):
                    n, G = N + U_XR + m, G0 + G_XR + m
                    weights_in(n)
                    free_main(G)
                    kw, mids = None, None
                    if m == 0:
                        kw = lambda a: pe.wait_ge(xlo, XT * stat + a + 1)
                        mids = {5: lambda: stat1(stat)}
                    if m == 1:
                        mids = {2: lambda: stat2(stat)}
                    acc(main[main_slot(G)], m, XT, xg_hi, xg_lo, k_wait=kw, mids=mids).then_inc(unit, 1)

                pe.wait_ge(rb_s, stat + 1)
                pe.wait_ge(evac, G0 + G_GT - 1)
                vs = main[main_slot(G0 + G_GT) ^ 1][:, 0, :]
                for u in range(MT):
                    weights_in(N + U_V + u)
                    for kk in range(2):
                        k = 2 * u + kk
                        for b, (ww, xx) in enumerate(((w_hi, xg_hi), (w_hi, xg_lo), (w_lo, xg_hi))):
                            for t in range(NCH + 1):
                                c = t * P if t < NCH else TOK - P
                                last = pe.matmul(vbank[t] if t < NCH else vs, xx[:, k, c:c + P],
                                                 ww[:, u, kk * WA:(kk + 1) * WA],
                                                 start=(k == 0 and b == 0), stop=(k == XT - 1 and b == 2))
                    last.then_inc(unit, 1)

                for m in range(MT):
                    n, G = N + U_GT + m, G0 + G_GT + m
                    weights_in(n)
                    free_main(G, first_after_v=m + 1 if m < 2 else 0, layer=l)
                    acc(main[main_slot(G)], m, XT, xg_hi, xg_lo).then_inc(unit, 1)
                    if m == 0:
                        pe.wait_ge(v_ev, (NCH + 1) * (l + 1))
                        pe.wait_ge(par_s, 9 * 16 * (l + 1))
                    else:
                        pe.wait_ge(ri_ev, 2 * (l * MT + m))
                    pe.wait_ge(lv, LV * l + LV_CONV * MT)
                    for g in range(2):
                        for q in range(2):
                            last = pe.matmul(aux[g][:, q, 0:HALF], bd[:, g, m, :],
                                             xc[:, m, q * HALF:(q + 1) * HALF], start=True, stop=True)
                    last.then_inc(ri, 1)

                for m in range(MT):
                    n, G = N + U_U + m, G0 + G_U + m
                    weights_in(n)
                    free_main(G)
                    acc(main[main_slot(G)], m, XT, xg_hi, xg_lo).then_inc(unit, 1)
                    if m == 0:
                        pe.wait_ge(vp, 2 * (NCH + 1) * (l + 1))
                        pe.wait_ge(mask_s, l + 1)
                    if m < 2:
                        pe.wait_ge(ri_ev, 2 * MT * (l + 1))
                    else:
                        pe.wait_ge(sg_ev, 2 * (l * MT + m - 1))
                    for c in range(NCH):
                        for j in range(2):
                            pe.matmul(aux[m % 2][HD * j:HD * (j + 1), 0, c * CHUNK:(c + 1) * CHUNK],
                                      vt[:, c, m * P + HD * j:m * P + HD * (j + 1)], ws[:, 2 * m + j, :],
                                      start=True, stop=True)
                    pe.matmul(aux[m % 2][:, 1, 0:NSAMP], vt[:, NCH, m * P:(m + 1) * P],
                              ident[:, P - NSAMP:P], start=True, stop=True).then_inc(sg, 1)

                n, G, par = N + U_OUT, G0 + G_OUT, main_slot(G0 + G_OUT)
                with pe.Fori(0, 2) as i:
                    for j in range(4):
                        weights_in(i * 4 + (n + j))
                        free_main(i * 4 + (G + j))
                        kw = None
                        if j == 0:
                            kw = lambda a: pe.wait_ge(hlo, l * HT + HT0 + a + 1)
                        acc(main[(par + j) % 2], j, XT, h_hi, h_lo,
                            order=[4, 5, 6, 7, 0, 1, 2, 3], k_wait=kw).then_inc(unit, 1)

                ffn(l, 1, U_F2, G_F2)

                stat = 4 * l + 3
                for u in range(4):
                    n = N + U_PP + u
                    weights_in(n)
                    if u == 0:
                        pe.wait_ge(p_v, l + 1)
                    if u == 2:
                        pe.wait_ge(pp_ev, 4 * l + 2)
                    if u % 2:
                        pe.wait_ge(evac, G0 + G_PP + u - 1)
                    for o in range(2):
                        last = acc((main if u % 2 else aux)[o if not u % 2 else (main_slot(G0 + G_PP) + o) % 2],
                                   n % SLOTS, 2, pe_hi, pe_lo, col0=2 * P * o)
                    last.then_inc(unit, 1)
                pe.wait_ge(pp_ev, 4 * l + 4)
                stat1(stat)
                n, G = N + U_PG, G0 + G_PG
                for j in range(XT):
                    weights_in(n + j)
                    free_main(G + j)
                    acc(main[main_slot(G + j)], j % SLOTS, XT, xg_hi, xg_lo,
                        k_wait=(lambda a: pe.wait_ge(xlo, XT * stat + a + 1)) if j == 0 else None,
                        mids={5: lambda: stat2(stat)} if j == 0 else None).then_inc(unit, 1)
            stat1(4 * DEPTH)
            stat2(4 * DEPTH)

        @block.scalar
        def _(act):
            def hi(n, s, wait_used=True):
                if isinstance(n, int) and n >= TOTAL:
                    return
                act.wait_ge(raw_in[s], (n + (SLOTS - s)) * (16 // SLOTS))
                if wait_used and n >= SLOTS:
                    act.wait_ge(unit, n - (SLOTS - 1))
                act.activation(w_hi[:, s, :], raw[:, s, :], ACT.Copy).then_inc(whi, 1)

            def prep(stat, o, wait, square=True, split=True):
                n = stat * XT + o
                wait()
                if split:
                    act.activation(xg_hi[:, o, :], x[:, o, :], ACT.Copy, scale=gain(stat, o)).then_inc(xhi, 1)
                if square:
                    if n >= 2:
                        act.wait_ge(ssum_s, n - 1)
                    act.activation(sq(n), x[:, o, :], ACT.Square).then_inc(sq_s, 1)

            def root(stat):
                act.wait_ge(st1, stat + 1)
                act.activation(std, aux[1][:, 0, 0:NCH + 1], ACT.Sqrt, scale=1.0 / DM, bias=eps).then_inc(std_s, 1)

            def function(G, func, src, dst):
                act.wait_ge(evac, G + 1)
                act.activation(dst, src, func).then_inc(f_s, 1)

            def split_hi(count, k):
                act.wait_ge(hf_s, count)
                act.activation(h_hi[:, bass.ds(k, 1), :], tmp[:, 3:4, :], ACT.Copy).then_inc(hhi, 1)

            def ffn(l, which, u0, g0):
                stat = 4 * l + 2 * which
                n, G, h = l * UNITS + u0, l * GROUPS + g0, l * HT + which * (HT0 + XT)
                root(stat)
                for c, tiles in enumerate(FFN_CHUNKS):
                    with act.Fori(0, tiles // 2) as i:
                        for j in range(2):
                            function(i * 4 + (G + 2 * j), ACT.Silu, T(0), T(1))
                            hi(i * 4 + (n + 2 * j + AHEAD), (2 * j + AHEAD) % 4, False)
                            split_hi(i * 2 + (h + j + 1), i * 2 + j)
                            hi(i * 4 + (n + 2 * j + 1 + AHEAD), (2 * j + 1 + AHEAD) % 4, False)
                    n, G, h = n + 2 * tiles, G + 2 * tiles + XT, h + tiles
                    for o in range(XT):
                        if c == 2:
                            prep(stat + 1, o, lambda: act.wait_ge(evac, l * GROUPS + g0 + FFN_UNITS - XT + o + 1))
                        hi(n + o + AHEAD, (o + AHEAD) % 4)
                    n += XT

            act.dma_start(vecs[:, :], vecs_in).then_inc(vec_s, 16)
            act.dma_start(x[:, :, :], x_in).then_inc(x_in_s, 16)
            act.wait_ge(vec_s, 16)
            act.wait_ge(x_in_s, 16)
            act.wait_ge(const_s, 7)
            for o in range(XT):
                prep(0, o, lambda: None)
                if o % 2 and o // 2 < AHEAD:
                    hi(o // 2, o // 2)
            act.wait_ge(lamv, 1)
            act.activation(lt[:, 1, :], lt[:, 0, :], ACT.Exp).then_inc(lama, 1)

            for l in range(DEPTH):
                N, G0 = l * UNITS, l * GROUPS
                ffn(l, 0, U_F1, G_F1)
                root(4 * l + 1)
                for m in range(MT):
                    hi(N + U_XR + m + AHEAD, (m + AHEAD) % 4)
                for u in range(MT - 1):
                    hi(N + U_V + u + AHEAD, (u + AHEAD) % 4)
                act.wait_ge(unit, N + U_GT)
                act.wait_ge(rb_s, 4 * l + 2)
                vs = main[main_slot(G0 + G_GT) ^ 1][:, 0, :]
                for t in range(NCH + 1):
                    act.activation(vt[:, t, :], vbank[t] if t < NCH else vs, ACT.Gelu_apprx_tanh,
                                   scale=rstd_t[:, t:t + 1]).then_inc(v_ev, 1)
                hi(N + U_GT + 2, 2)
                act.wait_ge(vn, VN * l + 2 * (NCH + 1))
                act.activation(vstd, mv[:, :, 1], ACT.Sqrt, bias=eps).then_inc(va, 1)
                for m in range(MT):
                    c = l * MT + m
                    function(G0 + G_GT + m, ACT.Gelu_apprx_tanh, gt[:, m, :], gt[:, m, :])
                    hi(N + U_GT + m + AHEAD, (m + AHEAD) % 4)
                    act.wait_ge(ri, c + 1)
                    act.activation(halves(T(0)), pair(aux[0]), ACT.Sigmoid, bias=vec(V_BR, l, m)).then_inc(ri_ev, 1)
                    act.activation(halves(T(1)), pair(aux[1]), ACT.Sigmoid, bias=vec(V_BI, l, m)).then_inc(ri_ev, 1)
                    act.wait_ge(ri_ev, 2 * c + 2)
                    if c == 0:
                        act.wait_ge(lamv, LAM_STEPS)
                    act.activation(T(2), T(0), ACT.Exp, scale=lam8[:, 0, c:c + 1]).then_inc(la, 1)
                    act.activation(T(5), T(0), ACT.Tanh, scale=lam8[:, 1, c:c + 1]).then_inc(la, 1)
                    act.wait_ge(lv, LV * l + LV_CONV * MT + LV_TILE * m + 4)
                    act.activation(T(5), T(4), ACT.Sqrt).then_inc(la, 1)
                    act.wait_ge(hf_s, l * HT + HT0 + m + 1)
                    act.activation(h_hi[:, MT + m, :], T(3), ACT.Copy).then_inc(hhi, 1)
                for m in range(MT):
                    function(G0 + G_U + m, ACT.Gelu_apprx_tanh, T(0), T(1))
                    hi(N + U_U + m + AHEAD, (m + AHEAD) % 4)
                    act.wait_ge(hf_s, l * HT + HT0 + MT + m + 1)
                    act.activation(h_hi[:, m, :], T(3), ACT.Copy).then_inc(hhi, 1)
                for o in range(XT):
                    prep(4 * l + 2, o, lambda: act.wait_ge(evac, G0 + G_OUT + o + 1))
                    hi(N + U_OUT + o + AHEAD, (o + AHEAD) % 4)
                act.wait_ge(p_s, 16 * (l + 1))
                act.activation(pe_hi[:, :, :].rearrange("p a b -> p (a b)"),
                               praw.rearrange("p a b -> p (a b)"), ACT.Copy).then_inc(p_a, 1)
                ffn(l, 1, U_F2, G_F2)
                for u in range(4):
                    hi(N + U_PP + u + AHEAD, (u + AHEAD) % 4)
                root(4 * l + 3)
                for o in range(XT):
                    function(G0 + G_PG + o, ACT.Sigmoid, T(0), T(1))
                    hi(N + U_PG + o + AHEAD, (o + AHEAD) % 4)
                    prep(4 * l + 4, o, lambda: act.wait_ge(x_new, l * XT + o + 1), split=False)
                if l + 1 < DEPTH:
                    act.wait_ge(unit, (l + 1) * UNITS)
                    for o in range(XT):
                        prep(4 * l + 4, o, lambda: None, square=False)
            root(4 * DEPTH)

        @block.vector
        def _(dve):
            def lo(n, s):
                if isinstance(n, int) and n >= TOTAL:
                    return
                dve.wait_ge(whi, n + 1)
                dve.tensor_tensor(w_lo[:, s, :], raw[:, s, :], w_hi[:, s, :], ALU.subtract).then_inc(wlo, 1)

            def x_lo(stat, o):
                dve.wait_ge(xhi, stat * XT + o + 1)
                dve.scalar_tensor_tensor(xg_lo[:, o, :], x[:, o, :], gain(stat, o), xg_hi[:, o, :],
                                         ALU.mult, ALU.subtract).then_inc(xlo, 1)

            def rstd_tok(stat):
                dve.wait_ge(std_s, stat + 1)
                dve.reciprocal(rstd_t, std).then_inc(rt_s, 1)
                dve.wait_ge(rt_s, stat + 1)
                dve.tensor_tensor(diag, ident[:, :].rearrange("p (a b) -> p a b", a=1).broadcast_to([P, NCH + 1, P]),
                                  rstd_t.rearrange("p (a b) -> p a b", b=1).broadcast_to([P, NCH + 1, P]),
                                  ALU.mult).then_inc(dg_s, 1)

            def rstd_all(stat):
                dve.wait_ge(st2, stat + 1)
                dve.tensor_copy(rstd_b[:, :], aux[0][:, :, :].rearrange("p a b -> p (a b)")[:, 0:TOK]).then_inc(rb_s, 1)
                dve.wait_ge(rb_s, stat + 1)

            def scaled(dst, g, sem_, u=None):
                dve.tensor_tensor(halves(dst), pair(main[g]), halves(rstd_b[:, :]), ALU.mult).then_inc(sem_, 1)

            def split_lo(count, k):
                dve.wait_ge(hhi, count)
                dve.tensor_tensor(h_lo[:, bass.ds(k, 1), :], tmp[:, 3:4, :], h_hi[:, bass.ds(k, 1), :],
                                  ALU.subtract).then_inc(hlo, 1)

            def ffn(l, which, u0, g0):
                stat = 4 * l + 2 * which
                n, G, h, g = l * UNITS + u0, l * GROUPS + g0, l * HT + which * (HT0 + XT), l * FS + which * (HT0 + FS_MIX)
                par = main_slot(G)
                rstd_tok(stat)
                rstd_all(stat)
                for c, tiles in enumerate(FFN_CHUNKS):
                    with dve.Fori(0, tiles // 2) as i:
                        for j in range(2):
                            dve.wait_ge(unit, i * 4 + (n + 2 * j + 1))
                            dve.tensor_tensor(halves(T(0)), pair(main[par]), halves(rstd_b[:, :]), ALU.mult).then_inc(evac, 1)
                            dve.wait_ge(evac, i * 4 + (G + 2 * j + 1))
                            lo(i * 4 + (n + 2 * j + AHEAD), (2 * j + AHEAD) % 4)
                            dve.wait_ge(unit, i * 4 + (n + 2 * j + 2))
                            dve.tensor_tensor(halves(T(2)), pair(main[1 - par]), halves(rstd_b[:, :]), ALU.mult).then_inc(evac, 1)
                            dve.wait_ge(evac, i * 4 + (G + 2 * j + 2))
                            dve.wait_ge(f_s, i * 2 + (g + j + 1))
                            dve.tensor_tensor(T(3), T(1), T(2), ALU.mult).then_inc(hf_s, 1)
                            split_lo(i * 2 + (h + j + 1), i * 2 + j)
                            lo(i * 4 + (n + 2 * j + 1 + AHEAD), (2 * j + 1 + AHEAD) % 4)
                    n, G, h, g = n + 2 * tiles, G + 2 * tiles, h + tiles, g + tiles
                    for o in range(XT):
                        dve.wait_ge(unit, n + o + 1)
                        dve.scalar_tensor_tensor(halves(x[:, o, :]), pair(main[(par + o) % 2]), 0.5,
                                                 halves(x[:, o, :]), ALU.mult, ALU.add).then_inc(evac, 1)
                        if c == 2:
                            x_lo(stat + 1, o)
                        lo(n + o + AHEAD, (o + AHEAD) % 4)
                    n, G = n + XT, G + XT

            dve.wait_ge(vec_s, 16)
            dve.wait_ge(x_in_s, 16)
            dve.wait_ge(const_s, 7)
            lo(0, 0)
            for o in range(XT):
                x_lo(0, o)
                if o % 2 and 1 <= o // 2 < AHEAD:
                    lo(o // 2, o // 2)

            step = [0]

            def lam(ins):
                step[0] += 1
                ins.then_inc(lamv, 1)
                dve.wait_ge(lamv, step[0])

            L = vecs[:, V_LAM:V_LAM + DEPTH * MT]
            lam(dve.scalar_tensor_tensor(lt[:, 0, :], L, -1.0, L, ALU.mult, ALU.min))
            dve.wait_ge(lama, 1)
            lam(dve.tensor_scalar(lt[:, 0, :], lt[:, 1, :], 2.0, None, ALU.add))
            lam(dve.reciprocal(lt[:, 2, :], lt[:, 0, :]))
            lam(dve.tensor_tensor(lt[:, 0, :], lt[:, 1, :], lt[:, 2, :], ALU.mult))
            lam(dve.tensor_tensor(lt[:, 1, :], lt[:, 0, :], lt[:, 0, :], ALU.mult))
            lam(dve.tensor_scalar(lt[:, 2, :], lt[:, 1, :], 1.0 / 17, 1.0 / 15, ALU.mult, ALU.add))
            for k in (13, 11, 9, 7, 5, 3, 1):
                lam(dve.tensor_tensor(lt[:, 3, :], lt[:, 2, :], lt[:, 1, :], ALU.mult))
                lam(dve.tensor_scalar(lt[:, 2, :], lt[:, 3, :], 1.0 / k, None, ALU.add))
            lam(dve.tensor_tensor(lt[:, 3, :], lt[:, 2, :], lt[:, 0, :], ALU.mult))
            lam(dve.tensor_scalar(lt[:, 1, :], L, -1.0, 0.0, ALU.mult, ALU.max))
            lam(dve.scalar_tensor_tensor(lt[:, 2, :], lt[:, 3, :], 2.0, lt[:, 1, :], ALU.mult, ALU.add))
            lam(dve.tensor_scalar(lam8[:, 1, :], lt[:, 2, :], LRU_C, None, ALU.mult))
            lam(dve.tensor_scalar(lam8[:, 0, :], lt[:, 2, :], -LRU_C, None, ALU.mult))
            assert step[0] == LAM_STEPS, step[0]

            for l in range(DEPTH):
                N, G0 = l * UNITS, l * GROUPS
                ffn(l, 0, U_F1, G_F1)

                rstd_tok(4 * l + 1)
                rstd_all(4 * l + 1)
                done = [LV * l]

                def lstep(ins):
                    done[0] += 1
                    ins.then_inc(lv, 1)
                    dve.wait_ge(lv, done[0])

                dve.wait_ge(par_s, 9 * 16 * (l + 1))
                for m in range(MT):
                    c = l * MT + m
                    b = m % 2
                    dve.wait_ge(unit, N + U_XR + m + 1)
                    if c >= 2:
                        dve.wait_ge(pst, 3 * (c - 1))
                    scaled(xr[:, b, CONV - 1:CONV - 1 + TOK], main_slot(G0 + G_XR + m), evac)
                    dve.wait_ge(evac, G0 + G_XR + m + 1)
                    lo(N + U_XR + m + AHEAD, (m + AHEAD) % 4)

                    def cw(k):
                        q = V_CW + c * CONV + k
                        return vecs[:, q:q + 1]
                    lstep(dve.tensor_scalar(xc[:, m, 0:SEQ], xr[:, b, 0:SEQ], cw(0), vec(V_CB, l, m), ALU.mult, ALU.add))
                    lstep(dve.tensor_scalar(xc[:, m, SEQ:TOK], sconv[:, m, 0, :], cw(0), vec(V_CB, l, m), ALU.mult, ALU.add))
                    for k in range(1, CONV):
                        lstep(dve.scalar_tensor_tensor(xc[:, m, 0:SEQ], xr[:, b, k:k + SEQ], cw(k), xc[:, m, 0:SEQ],
                                                       ALU.mult, ALU.add))
                        row = sconv[:, m, k, :] if k < CONV - 1 else xr[:, b, SEQ + CONV - 1:SEQ + CONV - 1 + NSAMP]
                        lstep(dve.scalar_tensor_tensor(xc[:, m, SEQ:TOK], row, cw(k), xc[:, m, SEQ:TOK],
                                                       ALU.mult, ALU.add))

                for u in range(MT - 1):
                    lo(N + U_V + u + AHEAD, (u + AHEAD) % 4)
                vdone = [VN * l]

                def vstep(ins, wait=True):
                    vdone[0] += 1
                    ins.then_inc(vn, 1)
                    if wait:
                        dve.wait_ge(vn, vdone[0])
                for t in range(NCH + 1):
                    dve.wait_ge(v_ev, (NCH + 1) * l + t + 1)
                    vstep(dve.bn_stats(bst[:, t, :], vt[:, t, :]))
                    vstep(dve.bn_aggr(mv[:, t, :], bst[:, t, :]))
                lo(N + U_GT + 2, 2)
                dve.wait_ge(va, l + 1)
                vstep(dve.reciprocal(vrstd, vstd))
                for t in range(NCH + 1):
                    vstep(dve.tensor_scalar(vt[:, t, :], vt[:, t, :], mv[:, t, 0:1], vrstd[:, t:t + 1],
                                            ALU.subtract, ALU.mult), wait=False)

                for m in range(MT):
                    c = l * MT + m
                    dve.wait_ge(unit, N + U_GT + m + 1)
                    scaled(gt[:, m, :], main_slot(G0 + G_GT + m), evac)
                    dve.wait_ge(evac, G0 + G_GT + m + 1)
                    lo(N + U_GT + m + AHEAD, (m + AHEAD) % 4)
                    dve.wait_ge(ri_ev, 2 * c + 2)
                    lstep(dve.tensor_tensor(T(1), T(1), xc[:, m, :], ALU.mult))
                    dve.wait_ge(la, 3 * c + 2)
                    lstep(dve.tensor_tensor(T(4), T(2), T(2), ALU.mult))
                    lstep(dve.scalar_tensor_tensor(T(4), T(4), 1.0, T(5), ALU.add, ALU.mult))
                    lstep(dve.tensor_scalar(T(4), T(4), 0.0, None, ALU.max))
                    dve.wait_ge(la, 3 * c + 3)
                    lstep(dve.tensor_tensor(T(1), T(1), T(5), ALU.mult))
                    lstep(dve.tensor_tensor_scan(T(0)[:, 0:SEQ], T(2)[:, 0:SEQ], T(1)[:, 0:SEQ], 0.0, ALU.mult, ALU.add))
                    lstep(dve.tensor_tensor(T(0)[:, SEQ:TOK], T(2)[:, SEQ:TOK], sh0[:, m, :], ALU.mult))
                    lstep(dve.tensor_tensor(T(0)[:, SEQ:TOK], T(0)[:, SEQ:TOK], T(1)[:, SEQ:TOK], ALU.add))
                    dve.tensor_copy(states[:, l, m, S_H:S_H + 1], T(0)[:, SEQ - 1:SEQ]).then_inc(stc, 1)
                    dve.tensor_copy(states[:, l, m, S_HS:S_HS + NSAMP], T(0)[:, SEQ:TOK]).then_inc(stc, 1)
                    dve.wait_ge(f_s, l * FS + HT0 + m + 1)
                    dve.tensor_tensor(T(3), T(0), gt[:, m, :], ALU.mult).then_inc(hf_s, 1)
                    split_lo(l * HT + HT0 + m + 1, MT + m)

                for m in range(MT):
                    c = l * MT + m
                    dve.wait_ge(unit, N + U_U + m + 1)
                    scaled(T(0), main_slot(G0 + G_U + m), evac)
                    dve.wait_ge(evac, G0 + G_U + m + 1)
                    lo(N + U_U + m + AHEAD, (m + AHEAD) % 4)
                    dve.wait_ge(sg, c + 1)
                    dve.tensor_tensor(T(2)[:, 0:SEQ].rearrange("p (n i) -> p n i", n=NCH),
                                      aux[m % 2][:, 0, :].rearrange("p (n i) -> p n i", n=NCH),
                                      bs[:, m:m + 1, :].broadcast_to([P, NCH, CHUNK]), ALU.add).then_inc(sg_ev, 1)
                    dve.tensor_scalar(T(2)[:, SEQ:TOK], aux[m % 2][:, 1, 0:NSAMP], vec(V_W00, l, m), vec(V_B00, l, m),
                                      ALU.mult, ALU.add).then_inc(sg_ev, 1)
                    dve.wait_ge(sg_ev, 2 * c + 2)
                    dve.wait_ge(f_s, l * FS + HT0 + MT + m + 1)
                    dve.tensor_tensor(T(3), T(1), T(2), ALU.mult).then_inc(hf_s, 1)
                    split_lo(l * HT + HT0 + MT + m + 1, m)

                for o in range(XT):
                    dve.wait_ge(unit, N + U_OUT + o + 1)
                    dve.tensor_tensor(halves(x[:, o, :]), pair(main[main_slot(G0 + G_OUT + o)]),
                                      halves(x[:, o, :]), ALU.add).then_inc(evac, 1)
                    x_lo(4 * l + 2, o)
                    lo(N + U_OUT + o + AHEAD, (o + AHEAD) % 4)

                dve.wait_ge(p_a, l + 1)
                dve.tensor_tensor(pe_lo[:, :, :].rearrange("p a b -> p (a b)"), praw.rearrange("p a b -> p (a b)"),
                                  pe_hi[:, :, :].rearrange("p a b -> p (a b)"), ALU.subtract).then_inc(p_v, 1)
                ffn(l, 1, U_F2, G_F2)

                for u in range(4):
                    dve.wait_ge(unit, N + U_PP + u + 1)
                    for o in range(2):
                        if u % 2:
                            src, s = main[(main_slot(G0 + G_PP) + o) % 2], evac
                        else:
                            src, s = aux[o], pp_ev
                        dve.tensor_copy(halves(proj[:, 2 * u + o, :]), pair(src)).then_inc(s, 1)
                    lo(N + U_PP + u + AHEAD, (u + AHEAD) % 4)
                rstd_tok(4 * l + 3)
                rstd_all(4 * l + 3)
                dve.wait_ge(pp_ev, 4 * (l + 1))
                for o in range(XT):
                    dve.wait_ge(unit, N + U_PG + o + 1)
                    scaled(T(0), main_slot(G0 + G_PG + o), evac)
                    dve.wait_ge(evac, G0 + G_PG + o + 1)
                    lo(N + U_PG + o + AHEAD, (o + AHEAD) % 4)
                    dve.wait_ge(f_s, l * FS + HT0 + FS_MIX + HT0 + o + 1)
                    dve.tensor_tensor(T(2), T(1), proj[:, o, :], ALU.mult).then_inc(x_tmp, 1)
                    dve.wait_ge(x_tmp, l * XT + o + 1)
                    dve.tensor_tensor(x[:, o, :], x[:, o, :], T(2), ALU.add).then_inc(x_new, 1)
                dve.wait_ge(x_new, (l + 1) * XT)
                if l + 1 < DEPTH:
                    for o in range(XT):
                        x_lo(4 * l + 4, o)
            rstd_tok(4 * DEPTH)
            rstd_all(4 * DEPTH)
            for o in range(XT):
                dve.scalar_tensor_tensor(x[:, o, :], x[:, o, :], vecs[:, V_GF + o:V_GF + o + 1], rstd_b[:, :],
                                         ALU.mult, ALU.mult).then_inc(y_s, 1)


def weight_stream(w):
    import numpy as np

    out = np.zeros((TOTAL, P, UNIT), np.float32)
    at = 0

    def put(block):
        nonlocal at
        out[at, :, :block.shape[1]] = block
        at += 1

    def columns(a, o, k0, kn):
        return a[k0 * P:(k0 + kn) * P, o * P:(o + 1) * P].reshape(kn, P, P).transpose(1, 0, 2).reshape(P, kn * P)

    def ffn(gate, up, down):
        f = 0
        for tiles in FFN_CHUNKS:
            for k in range(f, f + tiles):
                put(columns(gate, k, 0, XT))
                put(columns(up, k, 0, XT))
            for o in range(XT):
                put(columns(down, o, f, tiles))
            f += tiles

    for l in range(DEPTH):
        ffn(w["w_ffn1_gate"][l], w["w_ffn1_up"][l], w["w_ffn1_down"][l])
        w_in = w["w_in"][l]
        for m in range(MT):
            put(columns(w_in, 2 * MT + m, 0, XT))
        for u in range(MT):
            put(w_in[2 * u * P:2 * (u + 1) * P, WA:2 * WA].reshape(2, P, WA).transpose(1, 0, 2).reshape(P, 2 * WA))
        for m in range(MT):
            put(columns(w_in, 3 * MT + m, 0, XT))
        for m in range(MT):
            put(columns(w_in, m, 0, XT))
        for o in range(XT):
            put(columns(w["w_out"][l], o, 0, XT))
        ffn(w["w_ffn2_gate"][l], w["w_ffn2_up"][l], w["w_ffn2_down"][l])
        for u in range(XT // 2):
            pair = [columns(w["w_ple_proj"][l], 2 * u + o, 0, PLE // P) for o in range(2)]
            put(np.concatenate(pair, 1))
        for o in range(XT):
            put(columns(w["w_ple_gate"][l], o, 0, XT))
    assert at == TOTAL
    return out


def kernel(**inputs):
    import numpy as np
    import concourse.bacc as bacc
    from concourse.bass_utils import run_bass_kernel_spmd

    a = {k: np.asarray(v) for k, v in inputs.items()}

    def feature_tiles(v):
        return np.moveaxis(v.reshape(*v.shape[:-1], v.shape[-1] // P, P), -1, 0)

    def tokens(prompt, sample, tiles):
        rows = np.concatenate([prompt, sample], 0)
        return np.ascontiguousarray(rows.T.reshape(tiles, P, TOK).transpose(1, 0, 2))

    def per_head(v):
        return feature_tiles(np.repeat(v, HD, axis=1))

    gains = np.stack([a["n_ffn1"], a["n_mix"], a["n_ffn2"], a["n_ple"]], 1)
    vecs = np.concatenate([v.reshape(P, -1) for v in (
        feature_tiles(gains), feature_tiles(a["n_final"]), feature_tiles(a["lam"]),
        feature_tiles(a["b_r"]), feature_tiles(a["b_i"]),
        feature_tiles(a["conv_w"]).transpose(0, 1, 3, 2), feature_tiles(a["conv_b"]),
        per_head(a["w_s"][:, :, 0, 0]), per_head(a["b_s"][:, :, 0]))], 1)
    arrays = {
        "weights": weight_stream(a),
        "x_in": tokens(a["x_prompt"][0], a["x_sample"][:, 0], XT),
        "p_in": np.stack([tokens(a["p_prompt"][l, 0], a["p_sample"][l, :, 0], PLE // P) for l in range(DEPTH)]),
        "vecs": vecs,
        "ln": np.stack([np.broadcast_to(np.stack([a["ln_v_g"][l], a["ln_v_b"][l]]), (P, 2, WA))
                        for l in range(DEPTH)]),
        "bs": np.stack([np.repeat(a["b_s"][l].reshape(MT, 2, CHUNK), HD, axis=1).transpose(1, 0, 2)
                        for l in range(DEPTH)]),
        "ws": a["w_s"].transpose(0, 3, 1, 2),
        "bd": np.stack([a["w_r"], a["w_i"]], 1).reshape(DEPTH, 2, MT, 2, HD, HD).transpose(0, 3, 1, 4, 2, 5),
        "sconv": feature_tiles(a["state_conv"]).transpose(1, 0, 4, 3, 2).reshape(DEPTH, P, -1),
        "sh0": feature_tiles(a["state_h"]).transpose(1, 0, 3, 2).reshape(DEPTH, P, -1),
    }
    outs = {"y": (P, XT, TOK), "st": (P, DEPTH * MT * NS), "v": (DEPTH, NSAMP, WA)}

    nc = bacc.Bacc("TRN2", target_bir_lowering=False, num_devices=1)
    args = []
    for name in arrays:
        args.append(nc.dram_tensor(name + "_dram", arrays[name].shape, F32, kind="ExternalInput").ap())
    for name, shape in outs.items():
        args.append(nc.dram_tensor(name + "_out", shape, F32, kind="ExternalOutput").ap())
    trunk(nc, *args)
    given = {name + "_dram": np.ascontiguousarray(v) for name, v in arrays.items()}
    r = run_bass_kernel_spmd(nc, [given], core_ids=[0]).results[0]

    y = r["y_out"].transpose(1, 0, 2).reshape(DM, TOK).T
    v = r["v_out"]
    st = r["st_out"].reshape(P, DEPTH, MT, NS).transpose(1, 3, 2, 0).reshape(DEPTH, NS, WB)
    c = np.ascontiguousarray
    return (c(y[:SEQ][None]), c(y[SEQ:][:, None]), c(st[:, S_H][:, None]), c(st[:, S_C:S_C + 3][:, None]),
            c(st[:, S_HS:S_HS + NSAMP]),
            c(st[:, S_CS:].reshape(DEPTH, 3, NSAMP, WB).transpose(0, 2, 1, 3)), c(v[:, :, None]))
```

```python
from contextlib import ExitStack

import concourse.bass as bass
from concourse import mybir

F32 = mybir.dt.float32
F32R = mybir.dt.float32r
ALU = mybir.AluOpType
ACT = mybir.ActivationFunctionType

P = 128
DEPTH, SEQ, NSAMP, DM, DFF, PLE = 2, 512, 8, 1024, 2816, 256
WA = WB = 512
CONV = 4
CHUNK = 128
HD = 64
TOK = SEQ + NSAMP
HALF = TOK // 2
XT = DM // P
MT = WA // P
NCH = SEQ // CHUNK
EPS = 1e-6
LRU_C = 8.0
FFN_CHUNKS = (8, 8, 6)
assert sum(FFN_CHUNKS) * P == DFF
SLOTS = 4
UNIT = 8 * P
AHEAD = 3

V_AFTER = 3

FFN_UNITS = sum(2 * t + XT for t in FFN_CHUNKS)
U_F1 = 0
U_XR = U_F1 + FFN_UNITS
U_GT = U_XR + MT
U_V = U_GT + V_AFTER
U_U = U_GT + 2 * MT
U_OUT = U_U + MT
U_F2 = U_OUT + XT
U_PP = U_F2 + FFN_UNITS
U_PG = U_PP + XT // 2
UNITS = U_PG + XT
TOTAL = DEPTH * UNITS

G_F1 = 0
G_XR = G_F1 + FFN_UNITS
G_GT = G_XR + MT
G_U = G_GT + MT
G_OUT = G_U + MT
G_F2 = G_OUT + XT
G_PP = G_F2 + FFN_UNITS
G_PG = G_PP + XT // 2
GROUPS = G_PG + XT

HT0 = sum(FFN_CHUNKS)
HT = 2 * HT0 + XT
Y_ORDER = (MT, MT + 1, 0, MT + 2, 1, MT + 3, 2, 3)
FS_MIX = 2 * MT
FS = 2 * HT0 + FS_MIX + XT



def gate_unit(m):
    return U_GT + m if m < V_AFTER else U_V + MT + m - V_AFTER


V_G = 0
V_GF = V_G + DEPTH * 4 * XT
V_LAM = V_GF + XT
V_BR = V_LAM + DEPTH * MT
V_BI = V_BR + DEPTH * MT
V_CW = V_BI + DEPTH * MT
V_CB = V_CW + DEPTH * MT * CONV
V_W00 = V_CB + DEPTH * MT
V_B00 = V_W00 + DEPTH * MT
V_LG = V_B00 + DEPTH * MT
V_LB = V_LG + DEPTH * MT
NV = V_LB + DEPTH * MT

S_H, S_C, S_HS, S_CS = 0, 1, 4, 4 + NSAMP
NS = S_CS + 3 * NSAMP


def main_slot(g):
    layer, k = divmod(g, GROUPS)
    return (g + layer + (k >= G_GT + V_AFTER)) % 2


def trunk(nc, weights, x_in, p_in, vecs_in, ln_in, bs_in, ws_in, bd_in, sc_in, sh_in,
          y_out, st_out, v_out):
    ctx = ExitStack()
    with ctx:
        def sb(name, shape, dt=F32):
            return ctx.enter_context(nc.sbuf_tensor(name, shape, dt))

        def sem(name):
            return ctx.enter_context(nc.semaphore(name))

        x = sb("x", [P, XT, TOK])
        parts = [[sb(f"part{i}_{q}", [P, XT, TOK], F32R) for q in ("hi", "lo")] for i in range(2)]
        raw = sb("raw", [P, SLOTS, UNIT])
        w_hi = sb("w_hi", [P, SLOTS, UNIT], F32R)
        w_lo = sb("w_lo", [P, SLOTS, UNIT], F32R)
        pe_hi = sb("pe_hi", [P, 2, TOK], F32R)
        pe_lo = sb("pe_lo", [P, 2, TOK], F32R)
        rstd_b = sb("rstd_b", [P, TOK])
        tmp = sb("tmp", [P, 6, TOK])
        mix = sb("mix", [P, 2 * MT * TOK + 2 * (TOK + CONV - 1) + (NCH + 1) * WA])
        vecs = sb("vecs", [P, NV])
        ln = sb("ln", [P, 2, WA])
        bs = sb("bs", [P, MT, CHUNK])
        ws = sb("ws", [P, 2 * MT, CHUNK])
        bd = sb("bd", [P, 2, MT, P])
        sconv = sb("sconv", [P, MT, 3, NSAMP])
        sh0 = sb("sh0", [P, MT, NSAMP])
        states = sb("states", [P, DEPTH, MT, NS])
        ident = sb("ident", [P, P])
        ones = sb("ones", [P, P])
        small = sb("small", [P, 64])
        lam8 = sb("lam8", [P, 2, DEPTH * MT])
        lt = sb("lt", [P, 4, DEPTH * MT])

        def region(at, *dims):
            n = 1
            for d in dims:
                n *= d
            v = mix[:, at:at + n]
            return (v if len(dims) == 1 else v.rearrange("p (a b) -> p a b", a=dims[0])), at + n

        XRW = TOK + CONV - 1
        xc, at = region(0, MT, TOK)
        gt, at = region(at, MT, TOK)
        proj, _ = region(0, XT, TOK)
        xr, at = region(at, 2, XRW)
        praw, _ = region(at, 2, TOK)
        vt, at = region(at, NCH + 1, WA)
        rs = sb("rs", [P, 3, TOK])
        rs_sum = rs[:, 2, :]

        def sq(n):
            return rs[:, n % 2, :]

        SUMS = XT - 1

        VN = 2 * (NCH + 1) + 1 + (NCH + 1)

        def vn_tile(t):
            return 2 * (NCH + 1) + 1 + t + 1

        Y_DVE = XT - 2
        CS_STEPS = 2 * CONV - 1
        LAM_STEPS = 25
        eps = small[:, 0:1]
        rstd_t = small[:, 16:21]
        mv = small[:, 24:34].rearrange("p (a b) -> p a b", a=5)
        vstd = small[:, 34:39]
        vrstd = small[:, 40:45]
        scratch = small[:, 48:49]
        tap = small[:, 50:50 + NSAMP]
        bst = sb("bst", [P, 5, 6])

        main = [ctx.enter_context(nc.psum_tensor(f"main{i}", [P, 2, 512], F32)) for i in range(2)]
        aux = [ctx.enter_context(nc.psum_tensor(f"aux{i}", [P, 2, 512], F32)) for i in range(2)]
        vbank = [aux[0][:, 0, :], aux[0][:, 1, :], aux[1][:, 0, :], aux[1][:, 1, :]]

        raw_in = [sem(f"raw_in{s}") for s in range(SLOTS)]
        whi = sem("whi")
        wlo = sem("wlo")
        unit = sem("unit")
        evac = sem("evac")
        x_in_s = [sem(f"x_in{o}") for o in range(XT)]
        v_st = sem("v_st")
        x_tmp = sem("x_tmp")
        vec_s = sem("vec_s")
        par_s = sem("par_s")
        p_s = sem("p_s")
        const_s = sem("const_s")
        mask_s = sem("mask_s")
        lamv = sem("lamv")
        lama = sem("lama")
        sq_s = sem("sq_s")
        ssum_s = sem("ssum_s")
        xhi = sem("xhi")
        xlo = sem("xlo")
        x_new = sem("x_new")
        st1 = sem("st1")
        std_s = sem("std_s")
        rb_s = sem("rb_s")
        tm = sem("tm")
        rt_s = sem("rt_s")
        table_s = sem("table_s")
        f_s = sem("f_s")
        hf_s = sem("hf_s")
        hhi = sem("hhi")
        hlo = sem("hlo")
        ri = sem("ri")
        ri_ev = sem("ri_ev")
        ca_s = sem("ca_s")
        conv_s = sem("conv_s")
        cs_s = sem("cs_s")
        ix_s = sem("ix_s")
        la = sem("la")
        lw = sem("lw")
        lr = sem("lr")
        lh = sem("lh")
        bs_s = sem("bs_s")
        rsum = sem("rsum")
        vfm = sem("vfm")
        v_ev = sem("v_ev")
        vn = sem("vn")
        va = sem("va")
        vp = sem("vp")
        sg = sem("sg")
        sg_ev = sem("sg_ev")
        p_v = sem("p_v")
        p_a = sem("p_a")
        pp_ev = sem("pp_ev")
        stc = sem("stc")
        pst = sem("pst")
        y_s = sem("y_s")
        y_p = sem("y_p")
        yg = sem("yg")
        out_s = sem("out_s")

        def pair(ps):
            return ps[:, :, 0:HALF]

        def halves(ap):
            return ap.rearrange("p (a b) -> p a b", a=2)

        def T(k):
            return tmp[:, k, :]

        def xparts(l):
            return parts[l % 2]

        def hparts(l):
            return parts[1 - l % 2]

        lru = [T(4), T(5), xr[:, 0, CONV - 1:XRW], xr[:, 1, CONV - 1:XRW]]

        def gain(stat, o):
            return vecs[:, V_G + stat * XT + o:V_G + stat * XT + o + 1]

        def vec(base, layer, m):
            c = base + layer * MT + m
            return vecs[:, c:c + 1]

        def used(n):
            if isinstance(n, int) and U_PP <= n % UNITS < U_PG:
                return 2 * PLE
            return UNIT

        def add_square(eng, stat, o):
            n = stat * XT + o
            eng.wait_ge(sq_s, n + 1)
            if o == 1:
                if stat:
                    eng.wait_ge(st1, stat)
                eng.tensor_tensor(rs_sum, sq(n - 1), sq(n), ALU.add).then_inc(ssum_s, 1)
            else:
                eng.wait_ge(ssum_s, stat * SUMS + o - 1)
                eng.tensor_tensor(rs_sum, rs_sum, sq(n), ALU.add).then_inc(ssum_s, 1)

        block = ctx.enter_context(nc.Block())

        @block.sync
        def _(sp):
            sp.dma_start(vecs[:, :], vecs_in).then_inc(vec_s, 16)
            sp.dma_start(raw[:, 0, :], weights[0, :, :]).then_inc(raw_in[0], 16)
            for o in range(XT):
                sp.dma_start(x[:, o, :], x_in[:, o, :]).then_inc(x_in_s[o], 16)
            for n in range(1, SLOTS):
                sp.dma_start(raw[:, n, :], weights[n, :, :]).then_inc(raw_in[n], 16)
            with sp.Fori(1, TOTAL // SLOTS) as i:
                for s in range(SLOTS):
                    sp.wait_ge(wlo, i * SLOTS + (s - SLOTS + 1))
                    sp.dma_start(raw[:, s, :].rearrange("p (a n) -> p a n", a=1),
                                 weights[bass.ds(i * SLOTS + s, 1), :, :].rearrange("a p n -> p a n")
                                 ).then_inc(raw_in[s], 16)
            sp.wait_ge(stc, DEPTH * MT * 2)
            sp.wait_ge(pst, DEPTH * MT * 3)
            sp.dma_start(st_out, states[:, :, :, :].rearrange("p l m n -> p (l m n)")).then_inc(out_s, 16)
            for o in range(XT):
                if o < Y_DVE:
                    sp.wait_ge(y_s, o + 1)
                else:
                    sp.wait_ge(y_p, o - Y_DVE + 1)
                sp.dma_start(y_out[:, o, :], x[:, o, :]).then_inc(out_s, 16)
            sp.wait_ge(out_s, 16 * (1 + XT))

        @block.gpsimd
        def _(pool):
            pool.memset(ident[:, :], 0.0).then_inc(const_s, 1)
            pool.memset(ones[:, :], 1.0).then_inc(const_s, 1)
            pool.memset(small[:, :], EPS).then_inc(const_s, 1)
            pool.memset(bd[:, :, :, :], 0.0).then_inc(const_s, 1)
            for b in range(2):
                pool.memset(xr[:, b, 0:CONV - 1], 0.0).then_inc(const_s, 1)
            pool.wait_ge(const_s, 6)
            pool.affine_select(out=ident[:, :], in_=ident[:, :], compare_op=ALU.not_equal, fill=1.0,
                               base=0, pattern=[[-1, P]], channel_multiplier=1).then_inc(const_s, 1)

            def load_layer(l):
                if l > 0:
                    pool.wait_ge(hlo, HT * l - HT + HT0 + XT)
                    pool.wait_ge(sg_ev, 2 * MT * l)
                    pool.wait_ge(stc, MT * 2 * l)
                    pool.wait_ge(pst, MT * 3 * l)
                pool.dma_start(ln[:, :, :], ln_in[l]).then_inc(par_s, 16)
                pool.dma_start(bs[:, :, :], bs_in[l]).then_inc(par_s, 16)
                pool.dma_start(ws[:, :, :], ws_in[l]).then_inc(par_s, 16)
                pool.dma_start(sconv[:, :, :, :].rearrange("p m k b -> p (m k b)"), sc_in[l]).then_inc(par_s, 16)
                pool.dma_start(sh0[:, :, :].rearrange("p m b -> p (m b)"), sh_in[l]).then_inc(par_s, 16)
                for q in range(2):
                    for j in range(2):
                        pool.dma_start(bd[HD * j:HD * j + HD, q, :, HD * j:HD * j + HD],
                                       bd_in[l, j, q]).then_inc(par_s, 16)
                pool.wait_ge(par_s, 9 * 16 * (l + 1))
                pool.affine_select(out=ws[:, :, :], in_=ws[:, :, :], compare_op=ALU.is_ge, fill=0.0,
                                   base=0, pattern=[[0, 2 * MT], [1, CHUNK]],
                                   channel_multiplier=-1).then_inc(mask_s, 1)

            def sums(stat):
                for o in range(1, XT - 1 if stat == 4 * DEPTH else XT):
                    add_square(pool, stat, o)

            def conv_states(l):
                for m in range(MT):
                    c = l * MT + m
                    pool.wait_ge(evac, l * GROUPS + G_XR + m + 1)
                    xs = xr[:, m % 2, SEQ + CONV - 1:XRW]

                    def cw(k):
                        return vecs[:, V_CW + c * CONV + k:V_CW + c * CONV + k + 1]
                    pool.tensor_scalar(xc[:, m, SEQ:TOK], sconv[:, m, 0, :], cw(0), vec(V_CB, l, m),
                                       ALU.mult, ALU.add).then_inc(cs_s, 1)
                    for k in range(1, CONV):
                        pool.wait_ge(cs_s, c * CS_STEPS + 2 * k - 1)
                        pool.tensor_scalar(tap, sconv[:, m, k, :] if k < CONV - 1 else xs, cw(k), None,
                                           ALU.mult).then_inc(cs_s, 1)
                        pool.wait_ge(cs_s, c * CS_STEPS + 2 * k)
                        pool.tensor_tensor(xc[:, m, SEQ:TOK], xc[:, m, SEQ:TOK], tap, ALU.add).then_inc(cs_s, 1)
                    pool.tensor_copy(states[:, l, m, S_C:S_C + 3], xr[:, m % 2, SEQ:SEQ + 3]).then_inc(pst, 1)
                    pool.tensor_copy(states[:, l, m, S_CS:S_CS + 2 * NSAMP],
                                     sconv[:, m, 1:3, :].rearrange("p k b -> p (k b)")).then_inc(pst, 1)
                    pool.tensor_copy(states[:, l, m, S_CS + 2 * NSAMP:NS],
                                     xr[:, m % 2, SEQ + 3:SEQ + 3 + NSAMP]).then_inc(pst, 1)

            load_layer(0)
            for l in range(DEPTH):
                sums(4 * l + 1)
                conv_states(l)
                S = slice(P - 32, P)
                pool.wait_ge(vn, VN * l + vn_tile(NCH))
                pool.tensor_tensor(ln[S, 0, :], vt[S, NCH, :], ln[S, 0, :], ALU.mult).then_inc(vp, 1)
                pool.wait_ge(vp, 2 * l + 1)
                pool.tensor_tensor(ln[S, 0, :], ln[S, 0, :], ln[S, 1, :], ALU.add).then_inc(vp, 1)
                pool.wait_ge(vp, 2 * l + 2)
                pool.dma_start(v_out[l, :, :], ln[P - NSAMP:P, 0, :]).then_inc(v_st, 16)
                pool.wait_ge(v_st, 16 * (l + 1))
                pool.wait_ge(sg, MT * (l + 1))
                pool.dma_start(praw, p_in[l]).then_inc(p_s, 16)
                sums(4 * l + 2)
                if l + 1 < DEPTH:
                    load_layer(l + 1)
                sums(4 * l + 3)
                sums(4 * l + 4)
            pool.wait_ge(rb_s, 4 * DEPTH + 1)
            for o in range(Y_DVE, XT):
                pool.wait_ge(yg, o + 1)
                pool.tensor_tensor(x[:, o, :], proj[:, o, :], rstd_b[:, :], ALU.mult).then_inc(y_p, 1)

        @block.tensor
        def _(pe):
            def acc(ps, s, kts, hi, lo, order=None, k_wait=None, stop=None, mids=None, col0=0):
                order = order or range(kts)
                order = list(order)
                for a, k in enumerate(order):
                    if k_wait is not None:
                        k_wait(a)
                    w = slice(col0 + k * P, col0 + (k + 1) * P)
                    for b, (ww, xx) in enumerate(((w_hi, hi), (w_hi, lo), (w_lo, hi))):
                        for q in range(2):
                            last = pe.matmul(ps[:, q, 0:HALF], ww[:, s, w], xx[:, k, q * HALF:(q + 1) * HALF],
                                             start=(a == 0 and b == 0), stop=(a == kts - 1 and b == 2))
                    if mids and a in mids:
                        mids[a]()
                return last

            def weights_in(n):
                pe.wait_ge(wlo, n + 1)

            def free_main(G, first_after_v=0, layer=0):
                if first_after_v == 1:
                    pe.wait_ge(evac, G)
                elif first_after_v == 2:
                    pe.wait_ge(v_ev, (NCH + 1) * (layer + 1))
                else:
                    if not (isinstance(G, int) and G < 2):
                        pe.wait_ge(evac, G - 1)

            def stat1(stat):
                if stat == 0:
                    pe.wait_ge(const_s, 7)
                final = stat == 4 * DEPTH
                pe.wait_ge(ssum_s, SUMS * (stat + 1) - (1 if final else 0))
                for q in range(2):
                    last = pe.matmul(aux[1][:, q, 0:HALF], ones[:, :], rs_sum[:, q * HALF:(q + 1) * HALF],
                                     start=True, stop=not final)
                if final:
                    pe.wait_ge(sq_s, XT * (stat + 1))
                    for q in range(2):
                        last = pe.matmul(aux[1][:, q, 0:HALF], ones[:, :], sq(XT - 1)[:, q * HALF:(q + 1) * HALF],
                                         start=False, stop=True)
                last.then_inc(st1, 1)

            def ffn(l, which, u0, g0):
                stat = 4 * l + 2 * which
                n, G, h = l * UNITS + u0, l * GROUPS + g0, l * HT + which * (HT0 + XT)
                for c, tiles in enumerate(FFN_CHUNKS):
                    def up(n, G, par, first=False):
                        for j in range(2 * 2):
                            weights_in(n + j)
                            free_main(G + j)
                            kw, mids = None, None
                            if first and j == 0:
                                kw = lambda a: pe.wait_ge(xlo, XT * stat + a + 1)
                            if first and j == (stat == 0):
                                mids = {7 if stat else 2: lambda: stat1(stat)}
                            acc(main[(par + j) % 2], j, XT, *xparts(l), k_wait=kw,
                                mids=mids).then_inc(unit, 1)
                    par = main_slot(G)
                    start = 0
                    if c == 0:
                        up(n, G, par, True)
                        start = 1
                    with pe.Fori(start, tiles // 2) as i:
                        up(i * 4 + n, i * 4 + G, par)
                    n, G, h = n + 2 * tiles, G + 2 * tiles, h + tiles
                    with pe.Fori(0, 2) as i:
                        for j in range(4):
                            weights_in(i * 4 + (n + j))
                            free_main(i * 4 + (G + j))
                            kw = None
                            if j == 0:
                                kw = lambda a: pe.wait_ge(hlo, h - tiles + a + 1)
                            acc(main[(par + j) % 2], j, tiles, *hparts(l), k_wait=kw).then_inc(unit, 1)
                    n, G = n + XT, G + XT

            def lru_gates(l, m):
                pe.wait_ge(conv_s, (CONV - 1) * (l * MT + m + 1))
                pe.wait_ge(cs_s, CS_STEPS * (l * MT + m + 1))
                if m == 0:
                    pe.wait_ge(par_s, 9 * 16 * (l + 1))
                    pe.wait_ge(rt_s, l + 1)
                    pe.wait_ge(bs_s, MT * (l + 1))
                else:
                    pe.wait_ge(ri_ev, 2 * (l * MT + m))
                for g in range(2):
                    for q in range(2):
                        last = pe.matmul(aux[g][:, q, 0:HALF], bd[:, g, m, :],
                                         xc[:, m, q * HALF:(q + 1) * HALF], start=True, stop=True)
                last.then_inc(ri, 1)

            for l in range(DEPTH):
                N, G0 = l * UNITS, l * GROUPS
                x_hi, x_lo = xparts(l)
                ffn(l, 0, U_F1, G_F1)

                stat = 4 * l + 1
                for m in range(MT):
                    n, G = N + U_XR + m, G0 + G_XR + m
                    weights_in(n)
                    free_main(G)
                    kw, mids = None, None
                    if m == 0:
                        kw = lambda a: pe.wait_ge(xlo, XT * stat + a + 1)
                        mids = {7: lambda: stat1(stat)}
                    if m == 3:
                        mids = {6: lambda: lru_gates(l, 0)}
                    acc(main[main_slot(G)], m, XT, x_hi, x_lo, k_wait=kw, mids=mids).then_inc(unit, 1)
                    if m == 1:
                        pe.wait_ge(rb_s, stat + 1)
                        for t in range(NCH + 1):
                            c = t * P if t < NCH else TOK - P
                            last = pe.matmul(aux[0][:, 0, t:t + 1], rstd_b[:, c:c + P], ident[:, 0:1],
                                             start=True, stop=True)
                        last.then_inc(tm, 1)
                        pe.wait_ge(mask_s, l + 1)
                        for t in range(MT):
                            for j in range(2):
                                last = pe.matmul(aux[0][HD * j:HD * (j + 1), 1, t * CHUNK:(t + 1) * CHUNK],
                                                 ones[:, 0:HD], ws[:, 2 * t + j, :], start=True, stop=True)
                        last.then_inc(rsum, 1)

                def output_gate(m):
                    n, G = N + gate_unit(m), G0 + G_GT + m
                    weights_in(n)
                    free_main(G, first_after_v=m - V_AFTER + 1 if m >= V_AFTER else 0, layer=l)
                    acc(main[main_slot(G)], n % SLOTS, XT, x_hi, x_lo,
                        mids={6: lambda: lru_gates(l, m + 1)} if m < V_AFTER else None).then_inc(unit, 1)

                for m in range(V_AFTER):
                    output_gate(m)

                pe.wait_ge(ri_ev, 2 * MT * (l + 1))
                pe.wait_ge(evac, G0 + G_GT + V_AFTER - 1)
                vs = main[main_slot(G0 + G_GT + V_AFTER) ^ 1][:, 0, :]
                for u in range(MT):
                    weights_in(N + U_V + u)
                    for kk in range(2):
                        k = 2 * u + kk
                        for b, (ww, xx) in enumerate(((w_hi, x_hi), (w_hi, x_lo), (w_lo, x_hi))):
                            for t in range(NCH + 1):
                                c = t * P if t < NCH else TOK - P
                                last = pe.matmul(vbank[t] if t < NCH else vs, xx[:, k, c:c + P],
                                                 ww[:, (U_V + u) % SLOTS, kk * WA:(kk + 1) * WA],
                                                 start=(k == 0 and b == 0), stop=(k == XT - 1 and b == 2))
                    last.then_inc(unit, 1)

                for m in range(V_AFTER, MT):
                    output_gate(m)

                for m in range(MT):
                    n, G = N + U_U + m, G0 + G_U + m
                    weights_in(n)
                    free_main(G, first_after_v=MT - V_AFTER + m + 1, layer=l)
                    acc(main[main_slot(G)], m, XT, x_hi, x_lo).then_inc(unit, 1)
                    if m == 0:
                        pe.wait_ge(vn, VN * l + vn_tile(NCH))
                    if m >= 2:
                        pe.wait_ge(sg_ev, 2 * (l * MT + m - 1))
                    for c in range(NCH):
                        for j in range(2):
                            pe.matmul(aux[m % 2][HD * j:HD * (j + 1), 0, c * CHUNK:(c + 1) * CHUNK],
                                      vt[:, c, m * P + HD * j:m * P + HD * (j + 1)], ws[:, 2 * m + j, :],
                                      start=True, stop=True)
                    pe.matmul(aux[m % 2][:, 1, 0:NSAMP], vt[:, NCH, m * P:(m + 1) * P],
                              ident[:, P - NSAMP:P], start=True, stop=True).then_inc(sg, 1)

                n, G, par = N + U_OUT, G0 + G_OUT, main_slot(G0 + G_OUT)
                with pe.Fori(0, 2) as i:
                    for j in range(4):
                        weights_in(i * 4 + (n + j))
                        free_main(i * 4 + (G + j))
                        kw = None
                        if j == 0:
                            kw = lambda a: pe.wait_ge(hlo, l * HT + HT0 + a + 1)
                        acc(main[(par + j) % 2], j, XT, *hparts(l),
                            order=Y_ORDER, k_wait=kw).then_inc(unit, 1)

                ffn(l, 1, U_F2, G_F2)

                stat = 4 * l + 3
                for u in range(4):
                    n = N + U_PP + u
                    weights_in(n)
                    if u == 0:
                        pe.wait_ge(p_v, l + 1)
                    if u == 2:
                        pe.wait_ge(pp_ev, 4 * l + 2)
                    if u % 2:
                        pe.wait_ge(evac, G0 + G_PP + u - 1)
                    for o in range(2):
                        last = acc((main if u % 2 else aux)[o if not u % 2 else (main_slot(G0 + G_PP) + o) % 2],
                                   n % SLOTS, 2, pe_hi, pe_lo, col0=2 * P * o)
                    last.then_inc(unit, 1)
                pe.wait_ge(pp_ev, 4 * l + 4)
                stat1(stat)
                n, G = N + U_PG, G0 + G_PG
                for j in range(XT):
                    weights_in(n + j)
                    free_main(G + j)
                    acc(main[main_slot(G + j)], j % SLOTS, XT, x_hi, x_lo,
                        k_wait=(lambda a: pe.wait_ge(xlo, XT * stat + a + 1)) if j == 0 else None).then_inc(unit, 1)
            stat1(4 * DEPTH)

        @block.scalar
        def _(act):
            def hi(n, s, wait_used=True):
                if isinstance(n, int) and n >= TOTAL:
                    return
                act.wait_ge(raw_in[s], (n + (SLOTS - s)) * (16 // SLOTS))
                if wait_used and n >= SLOTS:
                    act.wait_ge(unit, n - (SLOTS - 1))
                c = used(n)
                act.activation(w_hi[:, s, 0:c], raw[:, s, 0:c], ACT.Copy).then_inc(whi, 1)

            def prep(stat, o):
                n = stat * XT + o
                if 0 < stat < 4 * DEPTH:
                    act.activation(xparts(stat // 4)[0][:, o, :], x[:, o, :], ACT.Copy,
                                   scale=gain(stat, o)).then_inc(xhi, 1)
                if o >= 2:
                    act.wait_ge(ssum_s, stat * SUMS + max(1, o - 2))
                act.activation(sq(n), x[:, o, :], ACT.Square).then_inc(sq_s, 1)
                if stat == 4 * DEPTH:
                    act.activation(proj[:, o, :], x[:, o, :], ACT.Copy,
                                   scale=vecs[:, V_GF + o:V_GF + o + 1]).then_inc(yg, 1)

            tables = [0]

            def table(func):
                if tables[0]:
                    act.wait_ge(table_s, tables[0])
                act.activation(scratch, eps, func).then_inc(table_s, 1)
                tables[0] += 1

            def root(stat):
                act.wait_ge(st1, stat + 1)
                act.activation(halves(rstd_b[:, :]), pair(aux[1]), ACT.Sqrt, scale=1.0 / DM, bias=eps).then_inc(std_s, 1)

            def function(G, func, src, dst):
                act.wait_ge(evac, G + 1)
                act.activation(dst, src, func).then_inc(f_s, 1)

            def split_hi(l, count, k):
                act.wait_ge(hf_s, count)
                act.activation(hparts(l)[0][:, bass.ds(k, 1), :], tmp[:, 3:4, :], ACT.Copy).then_inc(hhi, 1)

            def ffn(l, which, u0, g0):
                stat = 4 * l + 2 * which
                n, G, h = l * UNITS + u0, l * GROUPS + g0, l * HT + which * (HT0 + XT)
                root(stat)
                for c, tiles in enumerate(FFN_CHUNKS):
                    with act.Fori(0, tiles // 2) as i:
                        for j in range(2):
                            function(i * 4 + (G + 2 * j), ACT.Silu, T(0), T(1))
                            hi(i * 4 + (n + 2 * j + AHEAD), (2 * j + AHEAD) % 4, False)
                            split_hi(l, i * 2 + (h + j + 1), i * 2 + j)
                            hi(i * 4 + (n + 2 * j + 1 + AHEAD), (2 * j + 1 + AHEAD) % 4, False)
                    n, G, h = n + 2 * tiles, G + 2 * tiles + XT, h + tiles
                    if l == 0 and which == 0 and c == 0:
                        act.wait_ge(lamv, 1)
                        act.activation(lt[:, 1, :], lt[:, 0, :], ACT.Exp).then_inc(lama, 1)
                    for o in range(XT):
                        if c == 2:
                            act.wait_ge(evac, l * GROUPS + g0 + FFN_UNITS - XT + o + 1)
                            prep(stat + 1, o)
                        hi(n + o + AHEAD, (o + AHEAD) % 4)
                    n += XT

            act.wait_ge(const_s, 7)
            table(ACT.Copy)
            act.wait_ge(vec_s, 16)
            hi(0, 0)
            for o in range(XT):
                act.wait_ge(x_in_s[o], 16)
                act.activation(parts[0][0][:, o, :], x[:, o, :], ACT.Copy, scale=gain(0, o)).then_inc(xhi, 1)
                if o >= XT // 2:
                    prep(0, o - XT // 2)
            hi(1, 1)
            for o in range(XT // 2, XT):
                prep(0, o)
            hi(2, 2)

            for l in range(DEPTH):
                N, G0 = l * UNITS, l * GROUPS
                ffn(l, 0, U_F1, G_F1)
                root(4 * l + 1)
                def lru_sigmoids(m):
                    c = l * MT + m
                    act.wait_ge(ri, c + 1)
                    act.activation(halves(T(m)), pair(aux[0]), ACT.Sigmoid, bias=vec(V_BR, l, m)).then_inc(ri_ev, 1)
                    if m >= 2:
                        act.wait_ge(ix_s, c - 1)
                    act.activation(halves(sq(m)), pair(aux[1]), ACT.Sigmoid, bias=vec(V_BI, l, m)).then_inc(ri_ev, 1)

                def cut_y(count, src, k):
                    act.wait_ge(hf_s, count)
                    act.activation(hparts(l)[0][:, k, :], src, ACT.Copy).then_inc(hhi, 1)

                for m in range(MT):
                    act.wait_ge(evac, G0 + G_XR + m + 1)
                    c = l * MT + m
                    act.activation(xc[:, m, 0:SEQ], xr[:, m % 2, 0:SEQ], ACT.Identity, bias=vec(V_CB, l, m),
                                   scale=vecs[:, V_CW + c * CONV:V_CW + c * CONV + 1]).then_inc(ca_s, 1)
                    hi(N + U_XR + m + AHEAD, (U_XR + m + AHEAD) % SLOTS, False)
                    if m == 2:
                        table(ACT.Sigmoid)
                for m in range(V_AFTER):
                    lru_sigmoids(m)
                    hi(N + gate_unit(m) + AHEAD, (gate_unit(m) + AHEAD) % SLOTS)
                lru_sigmoids(MT - 1)
                if l == 0:
                    act.wait_ge(lamv, LAM_STEPS)
                act.wait_ge(ri_ev, 2 * MT * (l + 1))
                for m in range(MT):
                    c = l * MT + m
                    if m == 2:
                        act.wait_ge(pst, 3 * MT * (l + 1))
                    act.activation(lru[m], T(m), ACT.Tanh, scale=lam8[:, 1, c:c + 1])
                    act.activation(T(m), T(m), ACT.Exp, scale=lam8[:, 0, c:c + 1]).then_inc(la, 1)
                hi(N + U_V + AHEAD, (U_V + AHEAD) % SLOTS)
                for m in range(MT):
                    act.wait_ge(lw, 3 * (l * MT + m + 1))
                    act.activation(lru[m], lru[m], ACT.Sqrt).then_inc(lr, 1)
                hi(N + U_V + AHEAD + 1, (U_V + AHEAD + 1) % SLOTS)
                hi(N + U_V + AHEAD + 2, (U_V + AHEAD + 2) % SLOTS)
                table(ACT.Gelu_apprx_tanh)
                act.wait_ge(rt_s, l + 1)
                act.wait_ge(unit, N + U_V + MT)
                vs = main[main_slot(G0 + G_GT + V_AFTER) ^ 1][:, 0, :]
                for t in range(NCH + 1):
                    act.activation(vt[:, t, :], vbank[t] if t < NCH else vs, ACT.Gelu_apprx_tanh,
                                   scale=rstd_t[:, t:t + 1]).then_inc(v_ev, 1)
                table(ACT.Sqrt)
                hi(N + U_U + 1, (U_U + 1) % SLOTS)
                act.wait_ge(vn, VN * l + 2 * (NCH + 1))
                act.activation(vstd, mv[:, :, 1], ACT.Sqrt, bias=eps).then_inc(va, 1)
                for m in range(V_AFTER):
                    function(G0 + G_GT + m, ACT.Gelu_apprx_tanh, gt[:, m, :], gt[:, m, :])
                hi(N + U_U + 2, (U_U + 2) % SLOTS)
                for m in range(V_AFTER, MT):
                    function(G0 + G_GT + m, ACT.Gelu_apprx_tanh, gt[:, m, :], gt[:, m, :])
                for a, k in enumerate(Y_ORDER):
                    if k < MT:
                        function(G0 + G_U + k, ACT.Gelu_apprx_tanh, T(0), T(1))
                        hi(N + U_U + k + AHEAD, (k + AHEAD) % 4)
                    cut_y(l * HT + HT0 + a + 1, T(3) if k < MT else lru[k - MT], k)
                table(ACT.Sqrt)
                for o in range(XT):
                    act.wait_ge(evac, G0 + G_OUT + o + 1)
                    prep(4 * l + 2, o)
                    hi(N + U_OUT + o + AHEAD, (o + AHEAD) % 4)
                act.wait_ge(p_s, 16 * (l + 1))
                act.activation(pe_hi[:, :, :].rearrange("p a b -> p (a b)"),
                               praw.rearrange("p a b -> p (a b)"), ACT.Copy).then_inc(p_a, 1)
                ffn(l, 1, U_F2, G_F2)
                for u in range(4):
                    hi(N + U_PP + u + AHEAD, (u + AHEAD) % 4)
                    if u % 2 == 0:
                        act.wait_ge(unit, N + U_PP + u + 1)
                        for o in range(2):
                            act.activation(halves(proj[:, 2 * u + o, :]), pair(aux[o]), ACT.Copy).then_inc(pp_ev, 1)
                root(4 * l + 3)
                for o in range(XT):
                    function(G0 + G_PG + o, ACT.Sigmoid, T(0), T(1))
                    if o < XT - 1:
                        hi(N + U_PG + o + AHEAD, (o + AHEAD) % 4)
                    else:
                        table(ACT.Sqrt)
                    act.wait_ge(x_new, l * XT + o + 1)
                    prep(4 * l + 4, o)
                hi(N + U_PG + XT - 1 + AHEAD, (XT - 1 + AHEAD) % 4)
            root(4 * DEPTH)

        @block.vector
        def _(dve):
            def lo(n, s):
                if isinstance(n, int) and n >= TOTAL:
                    return
                dve.wait_ge(whi, n + 1)
                c = used(n)
                dve.tensor_tensor(w_lo[:, s, 0:c], raw[:, s, 0:c], w_hi[:, s, 0:c], ALU.subtract).then_inc(wlo, 1)

            def x_lo(stat, o):
                dve.wait_ge(xhi, stat * XT + o + 1)
                hi_, lo_ = xparts(stat // 4)
                dve.scalar_tensor_tensor(lo_[:, o, :], x[:, o, :], gain(stat, o), hi_[:, o, :],
                                         ALU.mult, ALU.subtract).then_inc(xlo, 1)

            def rstd(stat):
                dve.wait_ge(std_s, stat + 1)
                dve.reciprocal(rstd_b[:, :], rstd_b[:, :]).then_inc(rb_s, 1)
                dve.wait_ge(rb_s, stat + 1)

            def scaled(dst, g, sem_, u=None):
                dve.tensor_tensor(halves(dst), pair(main[g]), halves(rstd_b[:, :]), ALU.mult).then_inc(sem_, 1)

            def split_lo(l, count, k):
                dve.wait_ge(hhi, count)
                hi_, lo_ = hparts(l)
                dve.tensor_tensor(lo_[:, bass.ds(k, 1), :], tmp[:, 3:4, :], hi_[:, bass.ds(k, 1), :],
                                  ALU.subtract).then_inc(hlo, 1)

            def softplus():
                step = [0]

                def lam(ins):
                    step[0] += 1
                    ins.then_inc(lamv, 1)
                    dve.wait_ge(lamv, step[0])

                L = vecs[:, V_LAM:V_LAM + DEPTH * MT]
                lam(dve.scalar_tensor_tensor(lt[:, 0, :], L, -1.0, L, ALU.mult, ALU.min))
                dve.wait_ge(lama, 1)
                lam(dve.tensor_scalar(lt[:, 0, :], lt[:, 1, :], 2.0, None, ALU.add))
                lam(dve.reciprocal(lt[:, 2, :], lt[:, 0, :]))
                lam(dve.tensor_tensor(lt[:, 0, :], lt[:, 1, :], lt[:, 2, :], ALU.mult))
                lam(dve.tensor_tensor(lt[:, 1, :], lt[:, 0, :], lt[:, 0, :], ALU.mult))
                lam(dve.tensor_scalar(lt[:, 2, :], lt[:, 1, :], 1.0 / 17, 1.0 / 15, ALU.mult, ALU.add))
                for k in (13, 11, 9, 7, 5, 3, 1):
                    lam(dve.tensor_tensor(lt[:, 3, :], lt[:, 2, :], lt[:, 1, :], ALU.mult))
                    lam(dve.tensor_scalar(lt[:, 2, :], lt[:, 3, :], 1.0 / k, None, ALU.add))
                lam(dve.tensor_tensor(lt[:, 3, :], lt[:, 2, :], lt[:, 0, :], ALU.mult))
                lam(dve.tensor_scalar(lt[:, 1, :], L, -1.0, 0.0, ALU.mult, ALU.max))
                lam(dve.scalar_tensor_tensor(lt[:, 2, :], lt[:, 3, :], 2.0, lt[:, 1, :], ALU.mult, ALU.add))
                lam(dve.tensor_scalar(lam8[:, 1, :], lt[:, 2, :], LRU_C, None, ALU.mult))
                lam(dve.tensor_scalar(lam8[:, 0, :], lt[:, 2, :], -LRU_C, None, ALU.mult))
                assert step[0] == LAM_STEPS, step[0]

            def ffn(l, which, u0, g0):
                stat = 4 * l + 2 * which
                n, G, h, g = l * UNITS + u0, l * GROUPS + g0, l * HT + which * (HT0 + XT), l * FS + which * (HT0 + FS_MIX)
                par = main_slot(G)
                rstd(stat)
                for c, tiles in enumerate(FFN_CHUNKS):
                    with dve.Fori(0, tiles // 2) as i:
                        for j in range(2):
                            dve.wait_ge(unit, i * 4 + (n + 2 * j + 1))
                            dve.tensor_tensor(halves(T(0)), pair(main[par]), halves(rstd_b[:, :]), ALU.mult).then_inc(evac, 1)
                            dve.wait_ge(evac, i * 4 + (G + 2 * j + 1))
                            lo(i * 4 + (n + 2 * j + AHEAD), (2 * j + AHEAD) % 4)
                            dve.wait_ge(unit, i * 4 + (n + 2 * j + 2))
                            dve.tensor_tensor(halves(T(2)), pair(main[1 - par]), halves(rstd_b[:, :]), ALU.mult).then_inc(evac, 1)
                            dve.wait_ge(evac, i * 4 + (G + 2 * j + 2))
                            dve.wait_ge(f_s, i * 2 + (g + j + 1))
                            dve.tensor_tensor(T(3), T(1), T(2), ALU.mult).then_inc(hf_s, 1)
                            split_lo(l, i * 2 + (h + j + 1), i * 2 + j)
                            lo(i * 4 + (n + 2 * j + 1 + AHEAD), (2 * j + 1 + AHEAD) % 4)
                    n, G, h, g = n + 2 * tiles, G + 2 * tiles, h + tiles, g + tiles
                    if l == 0 and which == 0 and c == 0:
                        softplus()
                    for o in range(XT):
                        dve.wait_ge(unit, n + o + 1)
                        dve.scalar_tensor_tensor(halves(x[:, o, :]), pair(main[(par + o) % 2]), 0.5,
                                                 halves(x[:, o, :]), ALU.mult, ALU.add).then_inc(evac, 1)
                        if c == 2:
                            x_lo(stat + 1, o)
                        lo(n + o + AHEAD, (o + AHEAD) % 4)
                    n, G = n + XT, G + XT

            dve.wait_ge(vec_s, 16)
            lo(0, 0)
            for o in range(XT):
                dve.wait_ge(x_in_s[o], 16)
                x_lo(0, o)
                if o > XT // 2:
                    add_square(dve, 0, o - XT // 2)
            lo(1, 1)
            for o in range(XT // 2, XT):
                add_square(dve, 0, o)
            lo(2, 2)
            dve.wait_ge(const_s, 7)

            for l in range(DEPTH):
                N, G0 = l * UNITS, l * GROUPS
                ffn(l, 0, U_F1, G_F1)

                rstd(4 * l + 1)
                def step(ins, sem_, count):
                    ins.then_inc(sem_, 1)
                    dve.wait_ge(sem_, count)

                def conv(m):
                    c, b = l * MT + m, m % 2
                    dve.wait_ge(ca_s, c + 1)
                    for k in range(1, CONV):
                        q = V_CW + c * CONV + k
                        step(dve.scalar_tensor_tensor(xc[:, m, 0:SEQ], xr[:, b, k:k + SEQ], vecs[:, q:q + 1],
                                                      xc[:, m, 0:SEQ], ALU.mult, ALU.add),
                             conv_s, c * (CONV - 1) + k)

                def i_x(m):
                    c = l * MT + m
                    dve.wait_ge(ri_ev, 2 * c + 2)
                    dve.tensor_tensor(xc[:, m, :], sq(m), xc[:, m, :], ALU.mult).then_inc(ix_s, 1)

                dve.wait_ge(par_s, 9 * 16 * (l + 1))
                for m in range(MT):
                    c = l * MT + m
                    b = m % 2
                    dve.wait_ge(unit, N + U_XR + m + 1)
                    if c >= 2:
                        dve.wait_ge(pst, 3 * (c - 1))
                    scaled(xr[:, b, CONV - 1:XRW], main_slot(G0 + G_XR + m), evac)
                    dve.wait_ge(evac, G0 + G_XR + m + 1)
                    conv(m)
                    lo(N + U_XR + m + AHEAD, (m + AHEAD) % SLOTS)
                    if m == 1:
                        dve.wait_ge(tm, l + 1)
                        dve.tensor_copy(rstd_t, aux[0][:, 0, 0:NCH + 1]).then_inc(rt_s, 1)
                        dve.wait_ge(rsum, l + 1)
                        for t in range(MT):
                            dve.scalar_tensor_tensor(bs[:, t, :], aux[0][:, 1, t * CHUNK:(t + 1) * CHUNK],
                                                     vec(V_LB, l, t), bs[:, t, :], ALU.mult, ALU.add).then_inc(bs_s, 1)
                for m in range(V_AFTER):
                    dve.wait_ge(unit, N + gate_unit(m) + 1)
                    scaled(gt[:, m, :], main_slot(G0 + G_GT + m), evac)
                    lo(N + gate_unit(m) + AHEAD, (gate_unit(m) + AHEAD) % SLOTS)
                    i_x(m)
                i_x(MT - 1)

                dve.wait_ge(ix_s, MT * (l + 1))
                for m in range(MT):
                    c = l * MT + m
                    dve.wait_ge(la, c + 1)
                    step(dve.tensor_tensor(sq(m), T(m), T(m), ALU.mult), lw, 3 * c + 1)
                    step(dve.scalar_tensor_tensor(lru[m], sq(m), 1.0, lru[m], ALU.add, ALU.mult), lw, 3 * c + 2)
                    dve.tensor_scalar(lru[m], lru[m], 0.0, None, ALU.max).then_inc(lw, 1)
                for m in range(MT):
                    c = l * MT + m
                    dve.wait_ge(lr, c + 1)
                    dve.wait_ge(ix_s, c + 1)
                    step(dve.tensor_tensor(xc[:, m, :], xc[:, m, :], lru[m], ALU.mult), lh, 4 * c + 1)
                    dve.tensor_tensor_scan(lru[m][:, 0:SEQ], T(m)[:, 0:SEQ], xc[:, m, 0:SEQ], 0.0,
                                           ALU.mult, ALU.add).then_inc(lh, 1)
                    step(dve.tensor_tensor(lru[m][:, SEQ:TOK], T(m)[:, SEQ:TOK], sh0[:, m, :], ALU.mult),
                         lh, 4 * c + 3)
                    step(dve.tensor_tensor(lru[m][:, SEQ:TOK], lru[m][:, SEQ:TOK], xc[:, m, SEQ:TOK], ALU.add),
                         lh, 4 * c + 4)
                    dve.tensor_copy(states[:, l, m, S_H:S_H + 1], lru[m][:, SEQ - 1:SEQ]).then_inc(stc, 1)
                    dve.tensor_copy(states[:, l, m, S_HS:S_HS + NSAMP], lru[m][:, SEQ:TOK]).then_inc(stc, 1)
                    if m % 2:
                        n = U_V + AHEAD + m // 2
                        lo(N + n, n % SLOTS)

                lo(N + U_V + AHEAD + 2, (U_V + AHEAD + 2) % SLOTS)

                vdone = [VN * l]

                def vstep(ins, wait=True):
                    vdone[0] += 1
                    ins.then_inc(vn, 1)
                    if wait:
                        dve.wait_ge(vn, vdone[0])
                for t in range(NCH + 1):
                    dve.wait_ge(v_ev, (NCH + 1) * l + t + 1)
                    vstep(dve.bn_stats(bst[:, t, :], vt[:, t, :]))
                    vstep(dve.bn_aggr(mv[:, t, :], bst[:, t, :]))
                lo(N + U_U + 1, (U_U + 1) % SLOTS)
                dve.wait_ge(va, l + 1)
                vstep(dve.reciprocal(vrstd, vstd))
                for t in range(NCH + 1):
                    vstep(dve.tensor_scalar(vt[:, t, :], vt[:, t, :], mv[:, t, 0:1], vrstd[:, t:t + 1],
                                            ALU.subtract, ALU.mult), wait=False)

                for m in range(V_AFTER, MT):
                    dve.wait_ge(unit, N + gate_unit(m) + 1)
                    scaled(gt[:, m, :], main_slot(G0 + G_GT + m), evac)
                lo(N + U_U + 2, (U_U + 2) % SLOTS)

                def recurrent(m):
                    dve.wait_ge(f_s, l * FS + HT0 + m + 1)
                    dve.tensor_tensor(lru[m], lru[m], gt[:, m, :], ALU.mult).then_inc(hf_s, 1)

                def y_lo(k, src):
                    dve.wait_ge(hhi, l * HT + HT0 + Y_ORDER.index(k) + 1)
                    hi_, lo_ = hparts(l)
                    dve.tensor_tensor(lo_[:, k, :], src, hi_[:, k, :], ALU.subtract).then_inc(hlo, 1)

                recurrent(0)
                recurrent(1)
                y_lo(MT, lru[0])
                y_lo(MT + 1, lru[1])
                for m in range(MT):
                    c = l * MT + m
                    dve.wait_ge(unit, N + U_U + m + 1)
                    scaled(T(0), main_slot(G0 + G_U + m), evac)
                    if m in (1, 2):
                        y_lo(MT + m + 1, lru[m + 1])
                    dve.wait_ge(sg, c + 1)
                    dve.scalar_tensor_tensor(T(2)[:, 0:SEQ].rearrange("p (n i) -> p n i", n=NCH),
                                             aux[m % 2][:, 0, :].rearrange("p (n i) -> p n i", n=NCH), vec(V_LG, l, m),
                                             bs[:, m:m + 1, :].broadcast_to([P, NCH, CHUNK]),
                                             ALU.mult, ALU.add).then_inc(sg_ev, 1)
                    step(dve.tensor_scalar(T(2)[:, SEQ:TOK], aux[m % 2][:, 1, 0:NSAMP], vec(V_LG, l, m),
                                           vec(V_LB, l, m), ALU.mult, ALU.add), vfm, c + 1)
                    step(dve.tensor_scalar(T(2)[:, SEQ:TOK], T(2)[:, SEQ:TOK], vec(V_W00, l, m), vec(V_B00, l, m),
                                           ALU.mult, ALU.add), sg_ev, 2 * c + 2)
                    dve.wait_ge(f_s, l * FS + HT0 + MT + m + 1)
                    dve.tensor_tensor(T(3), T(1), T(2), ALU.mult).then_inc(hf_s, 1)
                    if m < 2:
                        recurrent(m + 2)
                    if m < MT - 1:
                        lo(N + U_U + m + AHEAD, (m + AHEAD) % SLOTS)
                    y_lo(m, T(3))
                lo(N + U_U + MT - 1 + AHEAD, (MT - 1 + AHEAD) % SLOTS)

                for o in range(XT):
                    dve.wait_ge(unit, N + U_OUT + o + 1)
                    dve.tensor_tensor(halves(x[:, o, :]), pair(main[main_slot(G0 + G_OUT + o)]),
                                      halves(x[:, o, :]), ALU.add).then_inc(evac, 1)
                    x_lo(4 * l + 2, o)
                    lo(N + U_OUT + o + AHEAD, (o + AHEAD) % 4)

                dve.wait_ge(p_a, l + 1)
                dve.tensor_tensor(pe_lo[:, :, :].rearrange("p a b -> p (a b)"), praw.rearrange("p a b -> p (a b)"),
                                  pe_hi[:, :, :].rearrange("p a b -> p (a b)"), ALU.subtract).then_inc(p_v, 1)
                ffn(l, 1, U_F2, G_F2)

                for u in range(4):
                    dve.wait_ge(unit, N + U_PP + u + 1)
                    for o in range(2 if u % 2 else 0):
                        dve.tensor_copy(halves(proj[:, 2 * u + o, :]),
                                        pair(main[(main_slot(G0 + G_PP) + o) % 2])).then_inc(evac, 1)
                    lo(N + U_PP + u + AHEAD, (u + AHEAD) % SLOTS)
                rstd(4 * l + 3)
                dve.wait_ge(pp_ev, 4 * (l + 1))
                for o in range(XT):
                    dve.wait_ge(unit, N + U_PG + o + 1)
                    scaled(T(0), main_slot(G0 + G_PG + o), evac)
                    if o and l + 1 < DEPTH:
                        x_lo(4 * l + 4, o - 1)
                    if o < XT - 1:
                        lo(N + U_PG + o + AHEAD, (o + AHEAD) % 4)
                    dve.wait_ge(f_s, l * FS + HT0 + FS_MIX + HT0 + o + 1)
                    dve.tensor_tensor(T(2), T(1), proj[:, o, :], ALU.mult).then_inc(x_tmp, 1)
                    dve.wait_ge(x_tmp, l * XT + o + 1)
                    dve.tensor_tensor(x[:, o, :], x[:, o, :], T(2), ALU.add).then_inc(x_new, 1)
                if l + 1 < DEPTH:
                    x_lo(4 * l + 4, XT - 1)
                lo(N + U_PG + XT - 1 + AHEAD, (XT - 1 + AHEAD) % 4)
            rstd(4 * DEPTH)
            dve.wait_ge(yg, Y_DVE)
            for o in range(Y_DVE):
                dve.tensor_tensor(x[:, o, :], proj[:, o, :], rstd_b[:, :], ALU.mult).then_inc(y_s, 1)


def weight_stream(w):
    import numpy as np

    out = np.zeros((TOTAL, P, UNIT), np.float32)
    at = 0

    def put(block):
        nonlocal at
        out[at, :, :block.shape[1]] = block
        at += 1

    def columns(a, o, k0, kn):
        return a[k0 * P:(k0 + kn) * P, o * P:(o + 1) * P].reshape(kn, P, P).transpose(1, 0, 2).reshape(P, kn * P)

    def ffn(gate, up, down):
        f = 0
        for tiles in FFN_CHUNKS:
            for k in range(f, f + tiles):
                put(columns(gate, k, 0, XT))
                put(columns(up, k, 0, XT))
            for o in range(XT):
                put(columns(down, o, f, tiles))
            f += tiles

    for l in range(DEPTH):
        ffn(w["w_ffn1_gate"][l], w["w_ffn1_up"][l], w["w_ffn1_down"][l])
        w_in = w["w_in"][l]
        for m in range(MT):
            put(columns(w_in, 2 * MT + m, 0, XT))
        for m in range(V_AFTER):
            put(columns(w_in, 3 * MT + m, 0, XT))
        for u in range(MT):
            put(w_in[2 * u * P:2 * (u + 1) * P, WA:2 * WA].reshape(2, P, WA).transpose(1, 0, 2).reshape(P, 2 * WA))
        for m in range(V_AFTER, MT):
            put(columns(w_in, 3 * MT + m, 0, XT))
        for m in range(MT):
            put(columns(w_in, m, 0, XT))
        for o in range(XT):
            put(columns(w["w_out"][l], o, 0, XT))
        ffn(w["w_ffn2_gate"][l], w["w_ffn2_up"][l], w["w_ffn2_down"][l])
        for u in range(XT // 2):
            pair = [columns(w["w_ple_proj"][l], 2 * u + o, 0, PLE // P) for o in range(2)]
            put(np.concatenate(pair, 1))
        for o in range(XT):
            put(columns(w["w_ple_gate"][l], o, 0, XT))
    assert at == TOTAL
    return out


def kernel(**inputs):
    import numpy as np
    import concourse.bacc as bacc
    from concourse.bass_utils import run_bass_kernel_spmd

    a = {k: np.asarray(v) for k, v in inputs.items()}

    def feature_tiles(v):
        return np.moveaxis(v.reshape(*v.shape[:-1], v.shape[-1] // P, P), -1, 0)

    def tokens(prompt, sample, tiles):
        rows = np.concatenate([prompt, sample], 0)
        return np.ascontiguousarray(rows.T.reshape(tiles, P, TOK).transpose(1, 0, 2))

    def per_head(v):
        return feature_tiles(np.repeat(v, HD, axis=1))

    gains = np.stack([a["n_ffn1"], a["n_mix"], a["n_ffn2"], a["n_ple"]], 1)
    vecs = np.concatenate([v.reshape(P, -1) for v in (
        feature_tiles(gains), feature_tiles(a["n_final"]), feature_tiles(a["lam"]),
        feature_tiles(a["b_r"]), feature_tiles(a["b_i"]),
        feature_tiles(a["conv_w"]).transpose(0, 1, 3, 2), feature_tiles(a["conv_b"]),
        per_head(a["w_s"][:, :, 0, 0]), per_head(a["b_s"][:, :, 0]),
        feature_tiles(a["ln_v_g"]), feature_tiles(a["ln_v_b"]))], 1)
    arrays = {
        "weights": weight_stream(a),
        "x_in": tokens(a["x_prompt"][0], a["x_sample"][:, 0], XT),
        "p_in": np.stack([tokens(a["p_prompt"][l, 0], a["p_sample"][l, :, 0], PLE // P) for l in range(DEPTH)]),
        "vecs": vecs,
        "ln": np.stack([np.broadcast_to(np.stack([a["ln_v_g"][l], a["ln_v_b"][l]]), (P, 2, WA))
                        for l in range(DEPTH)]),
        "bs": np.stack([np.repeat(a["b_s"][l].reshape(MT, 2, CHUNK), HD, axis=1).transpose(1, 0, 2)
                        for l in range(DEPTH)]),
        "ws": a["w_s"].transpose(0, 3, 1, 2),
        "bd": np.stack([a["w_r"], a["w_i"]], 1).reshape(DEPTH, 2, MT, 2, HD, HD).transpose(0, 3, 1, 4, 2, 5),
        "sconv": feature_tiles(a["state_conv"]).transpose(1, 0, 4, 3, 2).reshape(DEPTH, P, -1),
        "sh0": feature_tiles(a["state_h"]).transpose(1, 0, 3, 2).reshape(DEPTH, P, -1),
    }
    outs = {"y": (P, XT, TOK), "st": (P, DEPTH * MT * NS), "v": (DEPTH, NSAMP, WA)}

    nc = bacc.Bacc("TRN2", target_bir_lowering=False, num_devices=1)
    args = []
    for name in arrays:
        args.append(nc.dram_tensor(name + "_dram", arrays[name].shape, F32, kind="ExternalInput").ap())
    for name, shape in outs.items():
        args.append(nc.dram_tensor(name + "_out", shape, F32, kind="ExternalOutput").ap())
    trunk(nc, *args)
    given = {name + "_dram": np.ascontiguousarray(v) for name, v in arrays.items()}
    r = run_bass_kernel_spmd(nc, [given], core_ids=[0]).results[0]

    y = r["y_out"].transpose(1, 0, 2).reshape(DM, TOK).T
    v = r["v_out"]
    st = r["st_out"].reshape(P, DEPTH, MT, NS).transpose(1, 3, 2, 0).reshape(DEPTH, NS, WB)
    c = np.ascontiguousarray
    return (c(y[:SEQ][None]), c(y[SEQ:][:, None]), c(st[:, S_H][:, None]), c(st[:, S_C:S_C + 3][:, None]),
            c(st[:, S_HS:S_HS + NSAMP]),
            c(st[:, S_CS:].reshape(DEPTH, 3, NSAMP, WB).transpose(0, 2, 1, 3)), c(v[:, :, None]))
```

```python
from contextlib import ExitStack

import concourse.bass as bass
from concourse import mybir

F32 = mybir.dt.float32
F32R = mybir.dt.float32r
ALU = mybir.AluOpType
ACT = mybir.ActivationFunctionType
AX = mybir.AxisListType

P = 128
DEPTH, SEQ, NSAMP, DM, DFF, PLE = 2, 512, 8, 1024, 2816, 256
WA = WB = 512
CONV = 4
CHUNK = 128
HD = 64
TOK = SEQ + NSAMP
HALF = TOK // 2
XT = DM // P
MT = WA // P
NCH = SEQ // CHUNK
EPS = 1e-6
LRU_C = 8.0
FFN_CHUNKS = (8, 8, 6)
assert sum(FFN_CHUNKS) * P == DFF
SLOTS = 4
UNIT = 8 * P
AHEAD = 3

V_AFTER = 3

FFN_UNITS = sum(2 * t + XT for t in FFN_CHUNKS)
U_F1 = 0
U_XR = U_F1 + FFN_UNITS
U_GT = U_XR + MT
U_V = U_GT + V_AFTER
U_U = U_GT + 2 * MT
U_OUT = U_U + MT
U_F2 = U_OUT + XT
U_PP = U_F2 + FFN_UNITS
U_PG = U_PP + XT // 2
UNITS = U_PG + XT
TOTAL = DEPTH * UNITS

G_F1 = 0
G_XR = G_F1 + FFN_UNITS
G_GT = G_XR + MT
G_U = G_GT + MT
G_OUT = G_U + MT
G_F2 = G_OUT + XT
G_PP = G_F2 + FFN_UNITS
G_PG = G_PP + XT // 2
GROUPS = G_PG + XT

HT0 = sum(FFN_CHUNKS)
HT = 2 * HT0 + XT
Y_ORDER = (MT, MT + 1, 0, MT + 2, 1, MT + 3, 2, 3)
FS_MIX = 2 * MT
FS = 2 * HT0 + FS_MIX + XT


def gate_unit(m):
    return U_GT + m if m < V_AFTER else U_V + MT + m - V_AFTER


V_G = 0
V_GF = V_G + DEPTH * 4 * XT
V_LAM = V_GF + XT
V_BR = V_LAM + DEPTH * MT
V_BI = V_BR + DEPTH * MT
V_CW = V_BI + DEPTH * MT
V_CB = V_CW + DEPTH * MT * CONV
V_W00 = V_CB + DEPTH * MT
V_B00 = V_W00 + DEPTH * MT
V_LG = V_B00 + DEPTH * MT
V_LB = V_LG + DEPTH * MT
NV = V_LB + DEPTH * MT

S_H, S_C, S_HS, S_CS = 0, 1, 4, 4 + NSAMP
NS = S_CS + 3 * NSAMP


def main_slot(g):
    layer, k = divmod(g, GROUPS)
    return (g + layer + (k >= G_GT + V_AFTER)) % 2


def trunk(nc, weights, x_in, p_in, vecs_in, ln_in, bs_in, ws_in, bd_in, sc_in, sh_in,
          y_out, st_out, v_out):
    ctx = ExitStack()
    with ctx:
        def sb(name, shape, dt=F32):
            return ctx.enter_context(nc.sbuf_tensor(name, shape, dt))

        def sem(name):
            return ctx.enter_context(nc.semaphore(name))

        x = sb("x", [P, XT, TOK])
        parts = [[sb(f"part{i}_{q}", [P, XT, TOK], F32R) for q in ("hi", "lo")] for i in range(2)]
        raw = sb("raw", [P, SLOTS, UNIT])
        w_hi = sb("w_hi", [P, SLOTS, UNIT], F32R)
        w_lo = sb("w_lo", [P, SLOTS, UNIT], F32R)
        pe_hi = sb("pe_hi", [P, 2, TOK], F32R)
        pe_lo = sb("pe_lo", [P, 2, TOK], F32R)
        rstd_b = sb("rstd_b", [P, TOK])
        tmp = sb("tmp", [P, 6, TOK])
        mix = sb("mix", [P, 2 * MT * TOK + 2 * (TOK + CONV - 1) + (NCH + 1) * WA])
        vecs = sb("vecs", [P, NV])
        ln = sb("ln", [P, 2, WA])
        bs = sb("bs", [P, MT, CHUNK])
        ws = sb("ws", [P, 2 * MT, CHUNK])
        bd = sb("bd", [P, 2, MT, P])
        sconv = sb("sconv", [P, MT, 3, NSAMP])
        sh0 = sb("sh0", [P, MT, NSAMP])
        states = sb("states", [P, DEPTH, MT, NS])
        ident = sb("ident", [P, P])
        ones = sb("ones", [P, P])
        small = sb("small", [P, 64])
        lam8 = sb("lam8", [P, 2, DEPTH * MT])
        lt = sb("lt", [P, 4, DEPTH * MT])

        def region(at, *dims):
            n = 1
            for d in dims:
                n *= d
            v = mix[:, at:at + n]
            return (v if len(dims) == 1 else v.rearrange("p (a b) -> p a b", a=dims[0])), at + n

        XRW = TOK + CONV - 1
        xc, at = region(0, MT, TOK)
        gt, at = region(at, MT, TOK)
        proj, _ = region(0, XT, TOK)
        xr, at = region(at, 2, XRW)
        praw, _ = region(at, 2, TOK)
        vt, at = region(at, NCH + 1, WA)
        rs = sb("rs", [P, 3, TOK])
        rs_sum = rs[:, 2, :]

        def sq(n):
            return rs[:, n % 2, :]

        SUMS = XT - 1

        VN = 2 * (NCH + 1) + 1 + (NCH + 1)

        def vn_tile(t):
            return 2 * (NCH + 1) + 1 + t + 1

        Y_POOL = XT - 1
        CS_STEPS = 2 * CONV - 1
        LAM_STEPS = 25
        eps = small[:, 0:1]
        rstd_t = small[:, 16:21]
        mv = small[:, 24:34].rearrange("p (a b) -> p a b", a=5)
        vstd = small[:, 34:39]
        vrstd = small[:, 40:45]
        scratch = small[:, 48:49]
        tap = small[:, 50:50 + NSAMP]
        bst = sb("bst", [P, 5, 6])

        main = [ctx.enter_context(nc.psum_tensor(f"main{i}", [P, 2, 512], F32)) for i in range(2)]
        aux = [ctx.enter_context(nc.psum_tensor(f"aux{i}", [P, 2, 512], F32)) for i in range(2)]
        vbank = [aux[0][:, 0, :], aux[0][:, 1, :], aux[1][:, 0, :], aux[1][:, 1, :]]

        raw_in = [sem(f"raw_in{s}") for s in range(SLOTS)]
        whi = sem("whi")
        wlo = sem("wlo")
        unit = sem("unit")
        evac = sem("evac")
        x_in_s = [sem(f"x_in{o}") for o in range(XT // 2)]
        vec_s = sem("vec_s")
        par_s = sem("par_s")
        p_s = sem("p_s")
        const_s = sem("const_s")
        mask_s = sem("mask_s")
        lamv = sem("lamv")
        lama = sem("lama")
        sq_s = sem("sq_s")
        ssum_s = sem("ssum_s")
        xhi = sem("xhi")
        xlo = sem("xlo")
        x_tmp = sem("x_tmp")
        x_new = sem("x_new")
        st1 = sem("st1")
        std_s = sem("std_s")
        rb_s = sem("rb_s")
        rt_s = sem("rt_s")
        table_s = sem("table_s")
        f_s = sem("f_s")
        hf_s = sem("hf_s")
        hhi = sem("hhi")
        hlo = sem("hlo")
        ri = sem("ri")
        ri_ev = sem("ri_ev")
        ca_s = sem("ca_s")
        conv_s = sem("conv_s")
        cs_s = sem("cs_s")
        ix_s = sem("ix_s")
        la = sem("la")
        lw = sem("lw")
        lr = sem("lr")
        lh = sem("lh")
        bs_s = sem("bs_s")
        rsum = sem("rsum")
        vfm = sem("vfm")
        v_ev = sem("v_ev")
        vn = sem("vn")
        va = sem("va")
        vp = sem("vp")
        v_st = sem("v_st")
        sg = sem("sg")
        sg_ev = sem("sg_ev")
        p_a = sem("p_a")
        p_v = sem("p_v")
        pp_ev = sem("pp_ev")
        stc = sem("stc")
        pst = sem("pst")
        last_s = sem("last_s")
        last_ev = sem("last_ev")
        y_s = sem("y_s")
        y_p = sem("y_p")
        yg = sem("yg")
        out_s = sem("out_s")

        def pair(ps):
            return ps[:, :, 0:HALF]

        def halves(ap):
            return ap.rearrange("p (a b) -> p a b", a=2)

        def T(k):
            return tmp[:, k, :]

        def xparts(l):
            return parts[l % 2]

        def hparts(l):
            return parts[1 - l % 2]

        lru = [T(4), T(5), xr[:, 0, CONV - 1:XRW], xr[:, 1, CONV - 1:XRW]]

        def gain(stat, o):
            return vecs[:, V_G + stat * XT + o:V_G + stat * XT + o + 1]

        def vec(base, layer, m):
            c = base + layer * MT + m
            return vecs[:, c:c + 1]

        def used(n):
            if isinstance(n, int) and U_PP <= n % UNITS < U_PG:
                return 2 * PLE
            return UNIT

        def add_square(eng, stat, o):
            n = stat * XT + o
            eng.wait_ge(sq_s, n + 1)
            if o == 1:
                if stat:
                    eng.wait_ge(st1, stat)
                eng.tensor_tensor(rs_sum, sq(n - 1), sq(n), ALU.add).then_inc(ssum_s, 1)
            else:
                eng.wait_ge(ssum_s, stat * SUMS + o - 1)
                eng.tensor_tensor(rs_sum, rs_sum, sq(n), ALU.add).then_inc(ssum_s, 1)

        block = ctx.enter_context(nc.Block())

        @block.sync
        def _(sp):
            sp.dma_start(vecs[:, :], vecs_in).then_inc(vec_s, 16)
            sp.dma_start(raw[:, 0, :], weights[0, :, :]).then_inc(raw_in[0], 16)
            for o in range(0, XT, 2):
                sp.dma_start(x[:, o:o + 2, :], x_in[:, o:o + 2, :]).then_inc(x_in_s[o // 2], 16)
            for n in range(1, SLOTS):
                sp.dma_start(raw[:, n, :], weights[n, :, :]).then_inc(raw_in[n], 16)
            with sp.Fori(1, TOTAL // SLOTS) as i:
                for s in range(SLOTS):
                    sp.wait_ge(wlo, i * SLOTS + (s - SLOTS + 1))
                    sp.dma_start(raw[:, s, :].rearrange("p (a n) -> p a n", a=1),
                                 weights[bass.ds(i * SLOTS + s, 1), :, :].rearrange("a p n -> p a n")
                                 ).then_inc(raw_in[s], 16)
            sp.wait_ge(stc, DEPTH * MT * 2)
            sp.wait_ge(pst, DEPTH * MT * 3)
            sp.dma_start(st_out, states[:, :, :, :].rearrange("p l m n -> p (l m n)")).then_inc(out_s, 16)
            pieces = ((0, 0, 2, 2, 0), (1, 0, 2, 0, 3), (0, 2, 4, 4, 0), (1, 2, 4, 0, 5),
                      (0, 4, 6, 6, 0), (1, 4, 6, 0, 7), (0, 6, 8, 7, 1), (1, 6, 8, 0, 9))
            for q, o0, o1, by_pool, by_dve in pieces:
                if by_pool:
                    sp.wait_ge(y_p, by_pool)
                if by_dve:
                    sp.wait_ge(y_s, by_dve)
                h = slice(q * HALF, (q + 1) * HALF)
                sp.dma_start(y_out[:, o0:o1, h], x[:, o0:o1, h]).then_inc(out_s, 16)
            sp.wait_ge(out_s, 16 * (1 + len(pieces)))

        @block.gpsimd
        def _(pool):
            pool.memset(ident[:, :], 0.0).then_inc(const_s, 1)
            pool.memset(ones[:, :], 1.0).then_inc(const_s, 1)
            pool.memset(small[:, :], EPS).then_inc(const_s, 1)
            pool.memset(bd[:, :, :, :], 0.0).then_inc(const_s, 1)
            for b in range(2):
                pool.memset(xr[:, b, 0:CONV - 1], 0.0).then_inc(const_s, 1)
            pool.wait_ge(const_s, 6)
            pool.affine_select(out=ident[:, :], in_=ident[:, :], compare_op=ALU.not_equal, fill=1.0,
                               base=0, pattern=[[-1, P]], channel_multiplier=1).then_inc(const_s, 1)

            def load_layer(l):
                if l > 0:
                    pool.wait_ge(hlo, HT * l - HT + HT0 + XT)
                    pool.wait_ge(sg_ev, 2 * MT * l)
                    pool.wait_ge(stc, MT * 2 * l)
                    pool.wait_ge(pst, MT * 3 * l)
                pool.dma_start(ln[:, :, :], ln_in[l]).then_inc(par_s, 16)
                pool.dma_start(bs[:, :, :], bs_in[l]).then_inc(par_s, 16)
                pool.dma_start(ws[:, :, :], ws_in[l]).then_inc(par_s, 16)
                pool.dma_start(sconv[:, :, :, :].rearrange("p m k b -> p (m k b)"), sc_in[l]).then_inc(par_s, 16)
                pool.dma_start(sh0[:, :, :].rearrange("p m b -> p (m b)"), sh_in[l]).then_inc(par_s, 16)
                for q in range(2):
                    for j in range(2):
                        pool.dma_start(bd[HD * j:HD * j + HD, q, :, HD * j:HD * j + HD],
                                       bd_in[l, j, q]).then_inc(par_s, 16)
                pool.wait_ge(par_s, 9 * 16 * (l + 1))
                pool.affine_select(out=ws[:, :, :], in_=ws[:, :, :], compare_op=ALU.is_ge, fill=0.0,
                                   base=0, pattern=[[0, 2 * MT], [1, CHUNK]],
                                   channel_multiplier=-1).then_inc(mask_s, 1)

            def sums(stat):
                for o in range(1, XT - 1 if stat == 4 * DEPTH else XT):
                    add_square(pool, stat, o)

            def conv_states(l):
                for m in range(MT):
                    c = l * MT + m
                    pool.wait_ge(evac, l * GROUPS + G_XR + m + 1)
                    xs = xr[:, m % 2, SEQ + CONV - 1:XRW]

                    def cw(k):
                        return vecs[:, V_CW + c * CONV + k:V_CW + c * CONV + k + 1]
                    pool.tensor_scalar(xc[:, m, SEQ:TOK], sconv[:, m, 0, :], cw(0), vec(V_CB, l, m),
                                       ALU.mult, ALU.add).then_inc(cs_s, 1)
                    for k in range(1, CONV):
                        pool.wait_ge(cs_s, c * CS_STEPS + 2 * k - 1)
                        pool.tensor_scalar(tap, sconv[:, m, k, :] if k < CONV - 1 else xs, cw(k), None,
                                           ALU.mult).then_inc(cs_s, 1)
                        pool.wait_ge(cs_s, c * CS_STEPS + 2 * k)
                        pool.tensor_tensor(xc[:, m, SEQ:TOK], xc[:, m, SEQ:TOK], tap, ALU.add).then_inc(cs_s, 1)
                    pool.tensor_copy(states[:, l, m, S_C:S_C + 3], xr[:, m % 2, SEQ:SEQ + 3]).then_inc(pst, 1)
                    pool.tensor_copy(states[:, l, m, S_CS:S_CS + 2 * NSAMP],
                                     sconv[:, m, 1:3, :].rearrange("p k b -> p (k b)")).then_inc(pst, 1)
                    pool.tensor_copy(states[:, l, m, S_CS + 2 * NSAMP:NS],
                                     xr[:, m % 2, SEQ + 3:SEQ + 3 + NSAMP]).then_inc(pst, 1)

            load_layer(0)
            for l in range(DEPTH):
                sums(4 * l + 1)
                conv_states(l)
                S = slice(P - 32, P)
                pool.wait_ge(vn, VN * l + vn_tile(NCH))
                pool.tensor_tensor(ln[S, 0, :], vt[S, NCH, :], ln[S, 0, :], ALU.mult).then_inc(vp, 1)
                pool.wait_ge(vp, 2 * l + 1)
                pool.tensor_tensor(ln[S, 0, :], ln[S, 0, :], ln[S, 1, :], ALU.add).then_inc(vp, 1)
                pool.wait_ge(vp, 2 * l + 2)
                pool.dma_start(v_out[l, :, :], ln[P - NSAMP:P, 0, :]).then_inc(v_st, 16)
                pool.wait_ge(v_st, 16 * (l + 1))
                pool.wait_ge(sg, MT * (l + 1))
                pool.dma_start(praw, p_in[l]).then_inc(p_s, 16)
                sums(4 * l + 2)
                if l + 1 < DEPTH:
                    load_layer(l + 1)
                sums(4 * l + 3)
                sums(4 * l + 4)
            pool.wait_ge(rb_s, 4 * DEPTH + 1)
            pool.wait_ge(yg, Y_POOL)
            for o in range(Y_POOL):
                pool.tensor_tensor(x[:, o, 0:HALF], proj[:, o, 0:HALF], rstd_b[:, 0:HALF], ALU.mult).then_inc(y_p, 1)

        @block.tensor
        def _(pe):
            def acc(ps, s, kts, hi, lo, order=None, k_wait=None, mids=None, col0=0):
                for a, k in enumerate(order or range(kts)):
                    if k_wait is not None:
                        k_wait(a)
                    w = slice(col0 + k * P, col0 + (k + 1) * P)
                    for b, (ww, xx) in enumerate(((w_hi, hi), (w_hi, lo), (w_lo, hi))):
                        for q in range(2):
                            last = pe.matmul(ps[:, q, 0:HALF], ww[:, s, w], xx[:, k, q * HALF:(q + 1) * HALF],
                                             start=(a == 0 and b == 0), stop=(a == kts - 1 and b == 2))
                    if mids and a in mids:
                        mids[a]()
                return last

            def weights_in(n):
                pe.wait_ge(wlo, n + 1)

            def free_main(G, behind_v=0, layer=0):
                if behind_v == 1:
                    pe.wait_ge(evac, G)
                elif behind_v == 2:
                    pe.wait_ge(v_ev, (NCH + 1) * (layer + 1))
                elif not (isinstance(G, int) and G < 2):
                    pe.wait_ge(evac, G - 1)

            def stat1(stat):
                if stat == 0:
                    pe.wait_ge(const_s, 7)
                pe.wait_ge(ssum_s, SUMS * (stat + 1))
                for q in range(2):
                    last = pe.matmul(aux[1][:, q, 0:HALF], ones[:, :], rs_sum[:, q * HALF:(q + 1) * HALF],
                                     start=True, stop=True)
                last.then_inc(st1, 1)

            def ffn(l, which, u0, g0):
                stat = 4 * l + 2 * which
                n, G, h = l * UNITS + u0, l * GROUPS + g0, l * HT + which * (HT0 + XT)
                for c, tiles in enumerate(FFN_CHUNKS):
                    def up(n, G, par, first=False):
                        for j in range(2 * 2):
                            weights_in(n + j)
                            free_main(G + j)
                            kw, mids = None, None
                            if first and j == 0:
                                kw = lambda a: pe.wait_ge(xlo, XT * stat + a + 1)
                            if first and j == (stat == 0):
                                mids = {7 if stat else 2: lambda: stat1(stat)}
                            acc(main[(par + j) % 2], j, XT, *xparts(l), k_wait=kw,
                                mids=mids).then_inc(unit, 1)
                    par = main_slot(G)
                    start = 0
                    if c == 0:
                        up(n, G, par, True)
                        start = 1
                    with pe.Fori(start, tiles // 2) as i:
                        up(i * 4 + n, i * 4 + G, par)
                    n, G, h = n + 2 * tiles, G + 2 * tiles, h + tiles
                    with pe.Fori(0, 2) as i:
                        for j in range(4):
                            weights_in(i * 4 + (n + j))
                            free_main(i * 4 + (G + j))
                            kw = None
                            if j == 0:
                                kw = lambda a: pe.wait_ge(hlo, h - tiles + a + 1)
                            acc(main[(par + j) % 2], j, tiles, *hparts(l), k_wait=kw).then_inc(unit, 1)
                    n, G = n + XT, G + XT

            def lru_gates(l, m):
                pe.wait_ge(conv_s, (CONV - 1) * (l * MT + m + 1))
                pe.wait_ge(cs_s, CS_STEPS * (l * MT + m + 1))
                if m == 0:
                    pe.wait_ge(par_s, 9 * 16 * (l + 1))
                    pe.wait_ge(bs_s, MT * (l + 1))
                else:
                    pe.wait_ge(ri_ev, 2 * (l * MT + m))
                for g in range(2):
                    for q in range(2):
                        last = pe.matmul(aux[g][:, q, 0:HALF], bd[:, g, m, :],
                                         xc[:, m, q * HALF:(q + 1) * HALF], start=True, stop=True)
                last.then_inc(ri, 1)

            for l in range(DEPTH):
                N, G0 = l * UNITS, l * GROUPS
                x_hi, x_lo = xparts(l)
                ffn(l, 0, U_F1, G_F1)

                stat = 4 * l + 1
                for m in range(MT):
                    n, G = N + U_XR + m, G0 + G_XR + m
                    weights_in(n)
                    free_main(G)
                    kw, mids = None, None
                    if m == 0:
                        kw = lambda a: pe.wait_ge(xlo, XT * stat + a + 1)
                        mids = {7: lambda: stat1(stat)}
                    if m == 3:
                        mids = {6: lambda: lru_gates(l, 0)}
                    acc(main[main_slot(G)], m, XT, x_hi, x_lo, k_wait=kw, mids=mids).then_inc(unit, 1)
                    if m == 1:
                        pe.wait_ge(mask_s, l + 1)
                        for t in range(MT):
                            for j in range(2):
                                last = pe.matmul(aux[0][HD * j:HD * (j + 1), 1, t * CHUNK:(t + 1) * CHUNK],
                                                 ones[:, 0:HD], ws[:, 2 * t + j, :], start=True, stop=True)
                        last.then_inc(rsum, 1)

                def output_gate(m):
                    n, G = N + gate_unit(m), G0 + G_GT + m
                    weights_in(n)
                    free_main(G, behind_v=m - V_AFTER + 1 if m >= V_AFTER else 0, layer=l)
                    acc(main[main_slot(G)], n % SLOTS, XT, x_hi, x_lo,
                        mids={6 if m < V_AFTER - 1 else 4: lambda: lru_gates(l, m + 1)} if m < V_AFTER else None).then_inc(unit, 1)

                for m in range(V_AFTER):
                    output_gate(m)

                pe.wait_ge(ri_ev, 2 * MT * (l + 1))
                pe.wait_ge(evac, G0 + G_GT + V_AFTER - 1)
                vs = main[main_slot(G0 + G_GT + V_AFTER) ^ 1][:, 0, :]
                for u in range(MT):
                    weights_in(N + U_V + u)
                    for kk in range(2):
                        k = 2 * u + kk
                        for b, (ww, xx) in enumerate(((w_hi, x_hi), (w_hi, x_lo), (w_lo, x_hi))):
                            for t in range(NCH + 1):
                                c = t * P if t < NCH else TOK - P
                                last = pe.matmul(vbank[t] if t < NCH else vs, xx[:, k, c:c + P],
                                                 ww[:, (U_V + u) % SLOTS, kk * WA:(kk + 1) * WA],
                                                 start=(k == 0 and b == 0), stop=(k == XT - 1 and b == 2))
                    last.then_inc(unit, 1)

                for m in range(V_AFTER, MT):
                    output_gate(m)

                for m in range(MT):
                    n, G = N + U_U + m, G0 + G_U + m
                    weights_in(n)
                    free_main(G, behind_v=MT - V_AFTER + m + 1, layer=l)
                    acc(main[main_slot(G)], m, XT, x_hi, x_lo).then_inc(unit, 1)
                    if m == 0:
                        pe.wait_ge(vn, VN * l + vn_tile(NCH))
                    if m >= 2:
                        pe.wait_ge(sg_ev, 2 * (l * MT + m - 1))
                    for c in range(NCH):
                        for j in range(2):
                            pe.matmul(aux[m % 2][HD * j:HD * (j + 1), 0, c * CHUNK:(c + 1) * CHUNK],
                                      vt[:, c, m * P + HD * j:m * P + HD * (j + 1)], ws[:, 2 * m + j, :],
                                      start=True, stop=True)
                    pe.matmul(aux[m % 2][:, 1, 0:NSAMP], vt[:, NCH, m * P:(m + 1) * P],
                              ident[:, P - NSAMP:P], start=True, stop=True).then_inc(sg, 1)

                n, G, par = N + U_OUT, G0 + G_OUT, main_slot(G0 + G_OUT)
                with pe.Fori(0, 2) as i:
                    for j in range(4):
                        weights_in(i * 4 + (n + j))
                        free_main(i * 4 + (G + j))
                        kw = None
                        if j == 0:
                            kw = lambda a: pe.wait_ge(hlo, l * HT + HT0 + a + 1)
                        acc(main[(par + j) % 2], j, XT, *hparts(l),
                            order=Y_ORDER, k_wait=kw).then_inc(unit, 1)

                ffn(l, 1, U_F2, G_F2)

                stat = 4 * l + 3
                for u in range(4):
                    n = N + U_PP + u
                    weights_in(n)
                    if u == 0:
                        pe.wait_ge(p_v, l + 1)
                    if u == 2:
                        pe.wait_ge(pp_ev, 4 * l + 2)
                    if u % 2:
                        pe.wait_ge(evac, G0 + G_PP + u - 1)
                    for o in range(2):
                        last = acc((main if u % 2 else aux)[o if not u % 2 else (main_slot(G0 + G_PP) + o) % 2],
                                   n % SLOTS, 2, pe_hi, pe_lo, col0=2 * P * o)
                    last.then_inc(unit, 1)
                pe.wait_ge(pp_ev, 4 * l + 4)
                stat1(stat)
                n, G = N + U_PG, G0 + G_PG
                for j in range(XT if l + 1 < DEPTH else XT - 1):
                    weights_in(n + j)
                    free_main(G + j)
                    acc(main[main_slot(G + j)], j % SLOTS, XT, x_hi, x_lo,
                        k_wait=(lambda a: pe.wait_ge(xlo, XT * stat + a + 1)) if j == 0 else None).then_inc(unit, 1)

            weights_in(TOTAL - 1)
            free_main(G + XT - 1)
            s = (XT - 1) % SLOTS
            for q in range(2):
                for k in range(XT):
                    w = slice(k * P, (k + 1) * P)
                    for b, (ww, xx) in enumerate(((w_hi, x_hi), (w_hi, x_lo), (w_lo, x_hi))):
                        last = pe.matmul(main[main_slot(G + XT - 1)][:, q, 0:HALF], ww[:, s, w],
                                         xx[:, k, q * HALF:(q + 1) * HALF],
                                         start=(k == 0 and b == 0), stop=(k == XT - 1 and b == 2))
                last.then_inc(last_s, 1)
            pe.wait_ge(ssum_s, SUMS * (4 * DEPTH + 1) - 1)
            for q in range(2):
                h = slice(q * HALF, (q + 1) * HALF)
                pe.matmul(aux[1][:, q, 0:HALF], ones[:, :], rs_sum[:, h], start=True, stop=False)
                pe.wait_ge(sq_s, XT * (4 * DEPTH + 1) - 1 + q + 1)
                pe.matmul(aux[1][:, q, 0:HALF], ones[:, :], sq(XT - 1)[:, h], start=False, stop=True).then_inc(st1, 1)

        @block.scalar
        def _(act):
            def hi(n, s, wait_used=True):
                if isinstance(n, int) and n >= TOTAL:
                    return
                act.wait_ge(raw_in[s], (n + (SLOTS - s)) * (16 // SLOTS))
                if wait_used and n >= SLOTS:
                    act.wait_ge(unit, n - (SLOTS - 1))
                c = used(n)
                act.activation(w_hi[:, s, 0:c], raw[:, s, 0:c], ACT.Copy).then_inc(whi, 1)

            def prep(stat, o):
                n = stat * XT + o
                if 0 < stat < 4 * DEPTH:
                    act.activation(xparts(stat // 4)[0][:, o, :], x[:, o, :], ACT.Copy,
                                   scale=gain(stat, o)).then_inc(xhi, 1)
                if o >= 2:
                    act.wait_ge(ssum_s, stat * SUMS + max(1, o - 2))
                act.activation(sq(n), x[:, o, :], ACT.Square).then_inc(sq_s, 1)
                if stat == 4 * DEPTH:
                    act.activation(proj[:, o, :], x[:, o, :], ACT.Copy,
                                   scale=vecs[:, V_GF + o:V_GF + o + 1]).then_inc(yg, 1)

            tables = [0]

            def table(func):
                if tables[0]:
                    act.wait_ge(table_s, tables[0])
                act.activation(scratch, eps, func).then_inc(table_s, 1)
                tables[0] += 1

            def root(stat):
                act.wait_ge(st1, stat + 1)
                act.activation(halves(rstd_b[:, :]), pair(aux[1]), ACT.Sqrt, scale=1.0 / DM, bias=eps).then_inc(std_s, 1)

            def final_root(q):
                act.wait_ge(st1, 4 * DEPTH + 1 + q)
                act.activation(rstd_b[:, q * HALF:(q + 1) * HALF], aux[1][:, q, 0:HALF], ACT.Sqrt,
                               scale=1.0 / DM, bias=eps).then_inc(std_s, 1)

            def function(G, func, src, dst):
                act.wait_ge(evac, G + 1)
                act.activation(dst, src, func).then_inc(f_s, 1)

            def split_hi(l, count, k):
                act.wait_ge(hf_s, count)
                act.activation(hparts(l)[0][:, bass.ds(k, 1), :], tmp[:, 3:4, :], ACT.Copy).then_inc(hhi, 1)

            def ffn(l, which, u0, g0):
                stat = 4 * l + 2 * which
                n, G, h = l * UNITS + u0, l * GROUPS + g0, l * HT + which * (HT0 + XT)
                root(stat)
                for c, tiles in enumerate(FFN_CHUNKS):
                    with act.Fori(0, tiles // 2) as i:
                        for j in range(2):
                            function(i * 4 + (G + 2 * j), ACT.Silu, T(0), T(1))
                            hi(i * 4 + (n + 2 * j + AHEAD), (2 * j + AHEAD) % 4, False)
                            split_hi(l, i * 2 + (h + j + 1), i * 2 + j)
                            hi(i * 4 + (n + 2 * j + 1 + AHEAD), (2 * j + 1 + AHEAD) % 4, False)
                    n, G, h = n + 2 * tiles, G + 2 * tiles + XT, h + tiles
                    if l == 0 and which == 0 and c == 0:
                        act.wait_ge(lamv, 1)
                        act.activation(lt[:, 1, :], lt[:, 0, :], ACT.Exp).then_inc(lama, 1)
                    for o in range(XT):
                        if c == 2:
                            act.wait_ge(evac, l * GROUPS + g0 + FFN_UNITS - XT + o + 1)
                            prep(stat + 1, o)
                        hi(n + o + AHEAD, (o + AHEAD) % 4)
                    n += XT

            def lru_sigmoids(l, m):
                c = l * MT + m
                act.wait_ge(ri, c + 1)
                act.activation(halves(T(m)), pair(aux[0]), ACT.Sigmoid, bias=vec(V_BR, l, m)).then_inc(ri_ev, 1)
                if m >= 2:
                    act.wait_ge(ix_s, c - 1)
                act.activation(halves(sq(m)), pair(aux[1]), ACT.Sigmoid, bias=vec(V_BI, l, m)).then_inc(ri_ev, 1)

            def cut_y(l, a, src, k):
                act.wait_ge(hf_s, l * HT + HT0 + a + 1)
                act.activation(hparts(l)[0][:, k, :], src, ACT.Copy).then_inc(hhi, 1)

            act.wait_ge(const_s, 7)
            table(ACT.Copy)
            act.wait_ge(vec_s, 16)
            hi(0, 0)
            for o in range(XT):
                act.wait_ge(x_in_s[o // 2], 16)
                act.activation(parts[0][0][:, o, :], x[:, o, :], ACT.Copy, scale=gain(0, o)).then_inc(xhi, 1)
                if o >= XT // 2:
                    prep(0, o - XT // 2)
            hi(1, 1)
            for o in range(XT // 2, XT):
                prep(0, o)
            hi(2, 2)

            for l in range(DEPTH):
                N, G0 = l * UNITS, l * GROUPS
                ffn(l, 0, U_F1, G_F1)
                root(4 * l + 1)
                for m in range(MT):
                    if m == MT - 1:
                        lru_sigmoids(l, 0)
                    act.wait_ge(evac, G0 + G_XR + m + 1)
                    c = l * MT + m
                    act.activation(xc[:, m, 0:SEQ], xr[:, m % 2, 0:SEQ], ACT.Identity, bias=vec(V_CB, l, m),
                                   scale=vecs[:, V_CW + c * CONV:V_CW + c * CONV + 1]).then_inc(ca_s, 1)
                    hi(N + U_XR + m + AHEAD, (U_XR + m + AHEAD) % SLOTS, False)
                    if m == MT - 2:
                        table(ACT.Sigmoid)
                for m in range(V_AFTER):
                    hi(N + gate_unit(m) + AHEAD, (gate_unit(m) + AHEAD) % SLOTS)
                    lru_sigmoids(l, m + 1)
                if l == 0:
                    act.wait_ge(lamv, LAM_STEPS)
                act.wait_ge(ri_ev, 2 * MT * (l + 1))
                act.wait_ge(rt_s, 4 * (l + 1))
                for m in range(MT):
                    c = l * MT + m
                    if m == 2:
                        act.wait_ge(pst, 3 * MT * (l + 1))
                    act.activation(lru[m], T(m), ACT.Tanh, scale=lam8[:, 1, c:c + 1])
                    act.activation(T(m), T(m), ACT.Exp, scale=lam8[:, 0, c:c + 1]).then_inc(la, 1)
                hi(N + U_V + AHEAD, (U_V + AHEAD) % SLOTS)
                for m in range(MT):
                    act.wait_ge(lw, 3 * (l * MT + m + 1))
                    act.activation(lru[m], lru[m], ACT.Sqrt).then_inc(lr, 1)
                hi(N + U_V + AHEAD + 1, (U_V + AHEAD + 1) % SLOTS)
                hi(N + U_V + AHEAD + 2, (U_V + AHEAD + 2) % SLOTS)
                table(ACT.Gelu_apprx_tanh)
                act.wait_ge(unit, N + U_V + MT)
                vs = main[main_slot(G0 + G_GT + V_AFTER) ^ 1][:, 0, :]
                for t in range(NCH + 1):
                    act.activation(vt[:, t, :], vbank[t] if t < NCH else vs, ACT.Gelu_apprx_tanh,
                                   scale=rstd_t[:, t:t + 1]).then_inc(v_ev, 1)
                table(ACT.Sqrt)
                hi(N + U_U + 1, (U_U + 1) % SLOTS)
                act.wait_ge(vn, VN * l + 2 * (NCH + 1))
                act.activation(vstd, mv[:, :, 1], ACT.Sqrt, bias=eps).then_inc(va, 1)
                for m in range(V_AFTER):
                    function(G0 + G_GT + m, ACT.Gelu_apprx_tanh, gt[:, m, :], gt[:, m, :])
                hi(N + U_U + 2, (U_U + 2) % SLOTS)
                for m in range(V_AFTER, MT):
                    function(G0 + G_GT + m, ACT.Gelu_apprx_tanh, gt[:, m, :], gt[:, m, :])
                for a, k in enumerate(Y_ORDER):
                    if k < MT:
                        function(G0 + G_U + k, ACT.Gelu_apprx_tanh, T(0), T(1))
                        hi(N + U_U + k + AHEAD, (k + AHEAD) % 4)
                    cut_y(l, a, T(3) if k < MT else lru[k - MT], k)
                table(ACT.Sqrt)
                for o in range(XT):
                    act.wait_ge(evac, G0 + G_OUT + o + 1)
                    prep(4 * l + 2, o)
                    hi(N + U_OUT + o + AHEAD, (o + AHEAD) % 4)
                act.wait_ge(p_s, 16 * (l + 1))
                act.activation(pe_hi[:, :, :].rearrange("p a b -> p (a b)"),
                               praw.rearrange("p a b -> p (a b)"), ACT.Copy).then_inc(p_a, 1)
                ffn(l, 1, U_F2, G_F2)
                for u in range(4):
                    hi(N + U_PP + u + AHEAD, (u + AHEAD) % 4)
                    if u % 2 == 0:
                        act.wait_ge(unit, N + U_PP + u + 1)
                        for o in range(2):
                            act.activation(halves(proj[:, 2 * u + o, :]), pair(aux[o]), ACT.Copy).then_inc(pp_ev, 1)
                root(4 * l + 3)
                for o in range(XT if l + 1 < DEPTH else XT - 1):
                    function(G0 + G_PG + o, ACT.Sigmoid, T(0), T(1))
                    if o < XT - 1:
                        hi(N + U_PG + o + AHEAD, (o + AHEAD) % 4)
                    else:
                        table(ACT.Sqrt)
                    act.wait_ge(x_new, l * XT + o + 1)
                    prep(4 * l + 4, o)
                hi(N + U_PG + XT - 1 + AHEAD, (XT - 1 + AHEAD) % 4)

            act.wait_ge(ssum_s, SUMS * 4 * DEPTH + XT - 3)
            for q in range(2):
                h = slice(q * HALF, (q + 1) * HALF)
                act.wait_ge(last_ev, q + 1)
                act.activation(T(1)[:, h], T(0)[:, h], ACT.Sigmoid).then_inc(f_s, 1)
                if q:
                    table(ACT.Sqrt)
                    final_root(0)
                act.wait_ge(x_new, DEPTH * XT + q)
                act.activation(sq(XT - 1)[:, h], x[:, XT - 1, h], ACT.Square).then_inc(sq_s, 1)
            act.activation(proj[:, XT - 1, :], x[:, XT - 1, :], ACT.Copy,
                           scale=vecs[:, V_GF + XT - 1:V_GF + XT]).then_inc(yg, 1)
            final_root(1)

        @block.vector
        def _(dve):
            def lo(n, s):
                if isinstance(n, int) and n >= TOTAL:
                    return
                dve.wait_ge(whi, n + 1)
                c = used(n)
                dve.tensor_tensor(w_lo[:, s, 0:c], raw[:, s, 0:c], w_hi[:, s, 0:c], ALU.subtract).then_inc(wlo, 1)

            def x_lo(stat, o):
                dve.wait_ge(xhi, stat * XT + o + 1)
                hi_, lo_ = xparts(stat // 4)
                dve.scalar_tensor_tensor(lo_[:, o, :], x[:, o, :], gain(stat, o), hi_[:, o, :],
                                         ALU.mult, ALU.subtract).then_inc(xlo, 1)

            def rstd(stat):
                dve.wait_ge(std_s, stat + 1)
                dve.reciprocal(rstd_b[:, :], rstd_b[:, :]).then_inc(rb_s, 1)
                dve.wait_ge(rb_s, stat + 1)

            def scaled(dst, g, sem_):
                dve.tensor_tensor(halves(dst), pair(main[g]), halves(rstd_b[:, :]), ALU.mult).then_inc(sem_, 1)

            def split_lo(l, count, k):
                dve.wait_ge(hhi, count)
                hi_, lo_ = hparts(l)
                dve.tensor_tensor(lo_[:, bass.ds(k, 1), :], tmp[:, 3:4, :], hi_[:, bass.ds(k, 1), :],
                                  ALU.subtract).then_inc(hlo, 1)

            def softplus():
                step = [0]

                def lam(ins):
                    step[0] += 1
                    ins.then_inc(lamv, 1)
                    dve.wait_ge(lamv, step[0])

                L = vecs[:, V_LAM:V_LAM + DEPTH * MT]
                lam(dve.scalar_tensor_tensor(lt[:, 0, :], L, -1.0, L, ALU.mult, ALU.min))
                dve.wait_ge(lama, 1)
                lam(dve.tensor_scalar(lt[:, 0, :], lt[:, 1, :], 2.0, None, ALU.add))
                lam(dve.reciprocal(lt[:, 2, :], lt[:, 0, :]))
                lam(dve.tensor_tensor(lt[:, 0, :], lt[:, 1, :], lt[:, 2, :], ALU.mult))
                lam(dve.tensor_tensor(lt[:, 1, :], lt[:, 0, :], lt[:, 0, :], ALU.mult))
                lam(dve.tensor_scalar(lt[:, 2, :], lt[:, 1, :], 1.0 / 17, 1.0 / 15, ALU.mult, ALU.add))
                for k in (13, 11, 9, 7, 5, 3, 1):
                    lam(dve.tensor_tensor(lt[:, 3, :], lt[:, 2, :], lt[:, 1, :], ALU.mult))
                    lam(dve.tensor_scalar(lt[:, 2, :], lt[:, 3, :], 1.0 / k, None, ALU.add))
                lam(dve.tensor_tensor(lt[:, 3, :], lt[:, 2, :], lt[:, 0, :], ALU.mult))
                lam(dve.tensor_scalar(lt[:, 1, :], L, -1.0, 0.0, ALU.mult, ALU.max))
                lam(dve.scalar_tensor_tensor(lt[:, 2, :], lt[:, 3, :], 2.0, lt[:, 1, :], ALU.mult, ALU.add))
                lam(dve.tensor_scalar(lam8[:, 1, :], lt[:, 2, :], LRU_C, None, ALU.mult))
                lam(dve.tensor_scalar(lam8[:, 0, :], lt[:, 2, :], -LRU_C, None, ALU.mult))
                assert step[0] == LAM_STEPS, step[0]

            def ffn(l, which, u0, g0):
                stat = 4 * l + 2 * which
                n, G, h, g = l * UNITS + u0, l * GROUPS + g0, l * HT + which * (HT0 + XT), l * FS + which * (HT0 + FS_MIX)
                par = main_slot(G)
                rstd(stat)
                for c, tiles in enumerate(FFN_CHUNKS):
                    with dve.Fori(0, tiles // 2) as i:
                        for j in range(2):
                            dve.wait_ge(unit, i * 4 + (n + 2 * j + 1))
                            dve.tensor_tensor(halves(T(0)), pair(main[par]), halves(rstd_b[:, :]), ALU.mult).then_inc(evac, 1)
                            dve.wait_ge(evac, i * 4 + (G + 2 * j + 1))
                            lo(i * 4 + (n + 2 * j + AHEAD), (2 * j + AHEAD) % 4)
                            dve.wait_ge(unit, i * 4 + (n + 2 * j + 2))
                            dve.tensor_tensor(halves(T(2)), pair(main[1 - par]), halves(rstd_b[:, :]), ALU.mult).then_inc(evac, 1)
                            dve.wait_ge(evac, i * 4 + (G + 2 * j + 2))
                            dve.wait_ge(f_s, i * 2 + (g + j + 1))
                            dve.tensor_tensor(T(3), T(1), T(2), ALU.mult).then_inc(hf_s, 1)
                            split_lo(l, i * 2 + (h + j + 1), i * 2 + j)
                            lo(i * 4 + (n + 2 * j + 1 + AHEAD), (2 * j + 1 + AHEAD) % 4)
                    n, G, h, g = n + 2 * tiles, G + 2 * tiles, h + tiles, g + tiles
                    if l == 0 and which == 0 and c == 0:
                        softplus()
                    for o in range(XT):
                        dve.wait_ge(unit, n + o + 1)
                        dve.scalar_tensor_tensor(halves(x[:, o, :]), pair(main[(par + o) % 2]), 0.5,
                                                 halves(x[:, o, :]), ALU.mult, ALU.add).then_inc(evac, 1)
                        if c == 2:
                            x_lo(stat + 1, o)
                        lo(n + o + AHEAD, (o + AHEAD) % 4)
                    n, G = n + XT, G + XT

            def step(ins, sem_, count):
                ins.then_inc(sem_, 1)
                dve.wait_ge(sem_, count)

            def conv(l, m):
                c, b = l * MT + m, m % 2
                dve.wait_ge(ca_s, c + 1)
                for k in range(1, CONV):
                    q = V_CW + c * CONV + k
                    step(dve.scalar_tensor_tensor(xc[:, m, 0:SEQ], xr[:, b, k:k + SEQ], vecs[:, q:q + 1],
                                                  xc[:, m, 0:SEQ], ALU.mult, ALU.add),
                         conv_s, c * (CONV - 1) + k)

            def i_x(l, m):
                c = l * MT + m
                dve.wait_ge(ri_ev, 2 * c + 2)
                dve.tensor_tensor(xc[:, m, :], sq(m), xc[:, m, :], ALU.mult).then_inc(ix_s, 1)

            def recurrent(l, m):
                dve.wait_ge(f_s, l * FS + HT0 + m + 1)
                dve.tensor_tensor(lru[m], lru[m], gt[:, m, :], ALU.mult).then_inc(hf_s, 1)

            def y_lo(l, k, src):
                dve.wait_ge(hhi, l * HT + HT0 + Y_ORDER.index(k) + 1)
                hi_, lo_ = hparts(l)
                dve.tensor_tensor(lo_[:, k, :], src, hi_[:, k, :], ALU.subtract).then_inc(hlo, 1)

            dve.wait_ge(vec_s, 16)
            lo(0, 0)
            for o in range(XT):
                dve.wait_ge(x_in_s[o // 2], 16)
                x_lo(0, o)
                if o > XT // 2:
                    add_square(dve, 0, o - XT // 2)
            lo(1, 1)
            for o in range(XT // 2, XT):
                add_square(dve, 0, o)
            lo(2, 2)
            dve.wait_ge(const_s, 7)

            for l in range(DEPTH):
                N, G0 = l * UNITS, l * GROUPS
                ffn(l, 0, U_F1, G_F1)

                rstd(4 * l + 1)
                dve.wait_ge(par_s, 9 * 16 * (l + 1))
                for m in range(MT):
                    c = l * MT + m
                    b = m % 2
                    dve.wait_ge(unit, N + U_XR + m + 1)
                    if c >= 2:
                        dve.wait_ge(pst, 3 * (c - 1))
                    scaled(xr[:, b, CONV - 1:XRW], main_slot(G0 + G_XR + m), evac)
                    dve.wait_ge(evac, G0 + G_XR + m + 1)
                    conv(l, m)
                    lo(N + U_XR + m + AHEAD, (m + AHEAD) % SLOTS)
                    if m == 1:
                        dve.wait_ge(rsum, l + 1)
                        for t in range(MT):
                            dve.scalar_tensor_tensor(bs[:, t, :], aux[0][:, 1, t * CHUNK:(t + 1) * CHUNK],
                                                     vec(V_LB, l, t), bs[:, t, :], ALU.mult, ALU.add).then_inc(bs_s, 1)
                for m in range(V_AFTER):
                    dve.wait_ge(unit, N + gate_unit(m) + 1)
                    scaled(gt[:, m, :], main_slot(G0 + G_GT + m), evac)
                    lo(N + gate_unit(m) + AHEAD, (gate_unit(m) + AHEAD) % SLOTS)
                    i_x(l, m)
                    if m == 0:
                        blocks = T(4)[:, 0:SEQ].rearrange("p (t c) -> p t c", t=NCH)
                        dve.tensor_tensor(blocks, rstd_b[:, 0:SEQ].rearrange("p (t c) -> p t c", t=NCH),
                                          ident[:, :].rearrange("p (t c) -> p t c", t=1).broadcast_to([P, NCH, P]),
                                          ALU.mult).then_inc(rt_s, 1)
                        dve.tensor_tensor(T(5)[:, 0:P], rstd_b[:, TOK - P:TOK], ident[:, :],
                                          ALU.mult).then_inc(rt_s, 1)
                        dve.wait_ge(rt_s, 4 * l + 2)
                        dve.tensor_reduce(rstd_t[:, 0:NCH], blocks, AX.X, ALU.add).then_inc(rt_s, 1)
                        dve.tensor_reduce(rstd_t[:, NCH:NCH + 1], T(5)[:, 0:P], AX.X, ALU.add).then_inc(rt_s, 1)
                i_x(l, MT - 1)

                dve.wait_ge(ix_s, MT * (l + 1))
                for m in range(MT):
                    c = l * MT + m
                    dve.wait_ge(la, c + 1)
                    step(dve.tensor_tensor(sq(m), T(m), T(m), ALU.mult), lw, 3 * c + 1)
                    step(dve.scalar_tensor_tensor(lru[m], sq(m), 1.0, lru[m], ALU.add, ALU.mult), lw, 3 * c + 2)
                    dve.tensor_scalar(lru[m], lru[m], 0.0, None, ALU.max).then_inc(lw, 1)
                for m in range(MT):
                    c = l * MT + m
                    dve.wait_ge(lr, c + 1)
                    dve.wait_ge(ix_s, c + 1)
                    step(dve.tensor_tensor(xc[:, m, :], xc[:, m, :], lru[m], ALU.mult), lh, 4 * c + 1)
                    dve.tensor_tensor_scan(lru[m][:, 0:SEQ], T(m)[:, 0:SEQ], xc[:, m, 0:SEQ], 0.0,
                                           ALU.mult, ALU.add).then_inc(lh, 1)
                    step(dve.tensor_tensor(lru[m][:, SEQ:TOK], T(m)[:, SEQ:TOK], sh0[:, m, :], ALU.mult),
                         lh, 4 * c + 3)
                    step(dve.tensor_tensor(lru[m][:, SEQ:TOK], lru[m][:, SEQ:TOK], xc[:, m, SEQ:TOK], ALU.add),
                         lh, 4 * c + 4)
                    dve.tensor_copy(states[:, l, m, S_H:S_H + 1], lru[m][:, SEQ - 1:SEQ]).then_inc(stc, 1)
                    dve.tensor_copy(states[:, l, m, S_HS:S_HS + NSAMP], lru[m][:, SEQ:TOK]).then_inc(stc, 1)
                    if m % 2:
                        n = U_V + AHEAD + m // 2
                        lo(N + n, n % SLOTS)

                lo(N + U_V + AHEAD + 2, (U_V + AHEAD + 2) % SLOTS)

                for t in range(NCH + 1):
                    dve.wait_ge(v_ev, (NCH + 1) * l + t + 1)
                    step(dve.bn_stats(bst[:, t, :], vt[:, t, :]), vn, VN * l + 2 * t + 1)
                    step(dve.bn_aggr(mv[:, t, :], bst[:, t, :]), vn, VN * l + 2 * t + 2)
                lo(N + U_U + 1, (U_U + 1) % SLOTS)
                dve.wait_ge(va, l + 1)
                step(dve.reciprocal(vrstd, vstd), vn, VN * l + 2 * (NCH + 1) + 1)
                for t in range(NCH + 1):
                    dve.tensor_scalar(vt[:, t, :], vt[:, t, :], mv[:, t, 0:1], vrstd[:, t:t + 1],
                                      ALU.subtract, ALU.mult).then_inc(vn, 1)

                for m in range(V_AFTER, MT):
                    dve.wait_ge(unit, N + gate_unit(m) + 1)
                    scaled(gt[:, m, :], main_slot(G0 + G_GT + m), evac)
                lo(N + U_U + 2, (U_U + 2) % SLOTS)

                recurrent(l, 0)
                recurrent(l, 1)
                y_lo(l, MT, lru[0])
                y_lo(l, MT + 1, lru[1])
                for m in range(MT):
                    c = l * MT + m
                    dve.wait_ge(unit, N + U_U + m + 1)
                    scaled(T(0), main_slot(G0 + G_U + m), evac)
                    if m in (1, 2):
                        y_lo(l, MT + m + 1, lru[m + 1])
                    dve.wait_ge(sg, c + 1)
                    dve.scalar_tensor_tensor(T(2)[:, 0:SEQ].rearrange("p (n i) -> p n i", n=NCH),
                                             aux[m % 2][:, 0, :].rearrange("p (n i) -> p n i", n=NCH), vec(V_LG, l, m),
                                             bs[:, m:m + 1, :].broadcast_to([P, NCH, CHUNK]),
                                             ALU.mult, ALU.add).then_inc(sg_ev, 1)
                    step(dve.tensor_scalar(T(2)[:, SEQ:TOK], aux[m % 2][:, 1, 0:NSAMP], vec(V_LG, l, m),
                                           vec(V_LB, l, m), ALU.mult, ALU.add), vfm, c + 1)
                    step(dve.tensor_scalar(T(2)[:, SEQ:TOK], T(2)[:, SEQ:TOK], vec(V_W00, l, m), vec(V_B00, l, m),
                                           ALU.mult, ALU.add), sg_ev, 2 * c + 2)
                    dve.wait_ge(f_s, l * FS + HT0 + MT + m + 1)
                    dve.tensor_tensor(T(3), T(1), T(2), ALU.mult).then_inc(hf_s, 1)
                    if m < 2:
                        recurrent(l, m + 2)
                    if m < MT - 1:
                        lo(N + U_U + m + AHEAD, (m + AHEAD) % SLOTS)
                    y_lo(l, m, T(3))
                lo(N + U_U + MT - 1 + AHEAD, (MT - 1 + AHEAD) % SLOTS)

                for o in range(XT):
                    dve.wait_ge(unit, N + U_OUT + o + 1)
                    dve.tensor_tensor(halves(x[:, o, :]), pair(main[main_slot(G0 + G_OUT + o)]),
                                      halves(x[:, o, :]), ALU.add).then_inc(evac, 1)
                    x_lo(4 * l + 2, o)
                    lo(N + U_OUT + o + AHEAD, (o + AHEAD) % 4)

                dve.wait_ge(p_a, l + 1)
                dve.tensor_tensor(pe_lo[:, :, :].rearrange("p a b -> p (a b)"), praw.rearrange("p a b -> p (a b)"),
                                  pe_hi[:, :, :].rearrange("p a b -> p (a b)"), ALU.subtract).then_inc(p_v, 1)
                ffn(l, 1, U_F2, G_F2)

                for u in range(4):
                    dve.wait_ge(unit, N + U_PP + u + 1)
                    for o in range(2 if u % 2 else 0):
                        dve.tensor_copy(halves(proj[:, 2 * u + o, :]),
                                        pair(main[(main_slot(G0 + G_PP) + o) % 2])).then_inc(evac, 1)
                    lo(N + U_PP + u + AHEAD, (u + AHEAD) % SLOTS)
                rstd(4 * l + 3)
                dve.wait_ge(pp_ev, 4 * (l + 1))
                for o in range(XT if l + 1 < DEPTH else XT - 1):
                    dve.wait_ge(unit, N + U_PG + o + 1)
                    scaled(T(0), main_slot(G0 + G_PG + o), evac)
                    if o and l + 1 < DEPTH:
                        x_lo(4 * l + 4, o - 1)
                    if o < XT - 1:
                        lo(N + U_PG + o + AHEAD, (o + AHEAD) % 4)
                    dve.wait_ge(f_s, l * FS + HT0 + FS_MIX + HT0 + o + 1)
                    dve.tensor_tensor(T(2), T(1), proj[:, o, :], ALU.mult).then_inc(x_tmp, 1)
                    dve.wait_ge(x_tmp, l * XT + o + 1)
                    dve.tensor_tensor(x[:, o, :], x[:, o, :], T(2), ALU.add).then_inc(x_new, 1)
                if l + 1 < DEPTH:
                    x_lo(4 * l + 4, XT - 1)
                lo(N + U_PG + XT - 1 + AHEAD, (XT - 1 + AHEAD) % 4)
            o = XT - 1
            H = [slice(q * HALF, (q + 1) * HALF) for q in range(2)]
            for q in range(2):
                dve.wait_ge(last_s, q + 1)
                dve.tensor_tensor(T(0)[:, H[q]], main[main_slot(DEPTH * GROUPS - 1)][:, q, 0:HALF],
                                  rstd_b[:, H[q]], ALU.mult).then_inc(last_ev, 1)
                dve.wait_ge(f_s, DEPTH * FS + q)
                dve.tensor_tensor(T(2)[:, H[q]], T(1)[:, H[q]], proj[:, o, H[q]], ALU.mult).then_inc(x_tmp, 1)
                dve.wait_ge(x_tmp, DEPTH * XT + q)
                dve.tensor_tensor(x[:, o, H[q]], x[:, o, H[q]], T(2)[:, H[q]], ALU.add).then_inc(x_new, 1)
            for q in range(2):
                dve.wait_ge(std_s, 4 * DEPTH + 1 + q)
                dve.reciprocal(rstd_b[:, H[q]], rstd_b[:, H[q]]).then_inc(rb_s, 1)
            dve.wait_ge(rb_s, 4 * DEPTH + 2)
            dve.wait_ge(yg, XT)
            dve.tensor_tensor(x[:, o, H[0]], proj[:, o, H[0]], rstd_b[:, H[0]], ALU.mult).then_inc(y_s, 1)
            for o in range(XT):
                dve.tensor_tensor(x[:, o, H[1]], proj[:, o, H[1]], rstd_b[:, H[1]], ALU.mult).then_inc(y_s, 1)


def weight_stream(w):
    import numpy as np

    out = np.zeros((TOTAL, P, UNIT), np.float32)
    at = 0

    def put(block):
        nonlocal at
        out[at, :, :block.shape[1]] = block
        at += 1

    def columns(a, o, k0, kn):
        return a[k0 * P:(k0 + kn) * P, o * P:(o + 1) * P].reshape(kn, P, P).transpose(1, 0, 2).reshape(P, kn * P)

    def ffn(gate, up, down):
        f = 0
        for tiles in FFN_CHUNKS:
            for k in range(f, f + tiles):
                put(columns(gate, k, 0, XT))
                put(columns(up, k, 0, XT))
            for o in range(XT):
                put(columns(down, o, f, tiles))
            f += tiles

    for l in range(DEPTH):
        ffn(w["w_ffn1_gate"][l], w["w_ffn1_up"][l], w["w_ffn1_down"][l])
        w_in = w["w_in"][l]
        for m in range(MT):
            put(columns(w_in, 2 * MT + m, 0, XT))
        for m in range(V_AFTER):
            put(columns(w_in, 3 * MT + m, 0, XT))
        for u in range(MT):
            put(w_in[2 * u * P:2 * (u + 1) * P, WA:2 * WA].reshape(2, P, WA).transpose(1, 0, 2).reshape(P, 2 * WA))
        for m in range(V_AFTER, MT):
            put(columns(w_in, 3 * MT + m, 0, XT))
        for m in range(MT):
            put(columns(w_in, m, 0, XT))
        for o in range(XT):
            put(columns(w["w_out"][l], o, 0, XT))
        ffn(w["w_ffn2_gate"][l], w["w_ffn2_up"][l], w["w_ffn2_down"][l])
        for u in range(XT // 2):
            pair = [columns(w["w_ple_proj"][l], 2 * u + o, 0, PLE // P) for o in range(2)]
            put(np.concatenate(pair, 1))
        for o in range(XT):
            put(columns(w["w_ple_gate"][l], o, 0, XT))
    assert at == TOTAL
    return out


def kernel(**inputs):
    import numpy as np
    import concourse.bacc as bacc
    from concourse.bass_utils import run_bass_kernel_spmd

    a = {k: np.asarray(v) for k, v in inputs.items()}

    def feature_tiles(v):
        return np.moveaxis(v.reshape(*v.shape[:-1], v.shape[-1] // P, P), -1, 0)

    def tokens(prompt, sample, tiles):
        rows = np.concatenate([prompt, sample], 0)
        return np.ascontiguousarray(rows.T.reshape(tiles, P, TOK).transpose(1, 0, 2))

    def per_head(v):
        return feature_tiles(np.repeat(v, HD, axis=1))

    gains = np.stack([a["n_ffn1"], a["n_mix"], a["n_ffn2"], a["n_ple"]], 1)
    vecs = np.concatenate([v.reshape(P, -1) for v in (
        feature_tiles(gains), feature_tiles(a["n_final"]), feature_tiles(a["lam"]),
        feature_tiles(a["b_r"]), feature_tiles(a["b_i"]),
        feature_tiles(a["conv_w"]).transpose(0, 1, 3, 2), feature_tiles(a["conv_b"]),
        per_head(a["w_s"][:, :, 0, 0]), per_head(a["b_s"][:, :, 0]),
        feature_tiles(a["ln_v_g"]), feature_tiles(a["ln_v_b"]))], 1)
    arrays = {
        "weights": weight_stream(a),
        "x_in": tokens(a["x_prompt"][0], a["x_sample"][:, 0], XT),
        "p_in": np.stack([tokens(a["p_prompt"][l, 0], a["p_sample"][l, :, 0], PLE // P) for l in range(DEPTH)]),
        "vecs": vecs,
        "ln": np.stack([np.broadcast_to(np.stack([a["ln_v_g"][l], a["ln_v_b"][l]]), (P, 2, WA))
                        for l in range(DEPTH)]),
        "bs": np.stack([np.repeat(a["b_s"][l].reshape(MT, 2, CHUNK), HD, axis=1).transpose(1, 0, 2)
                        for l in range(DEPTH)]),
        "ws": a["w_s"].transpose(0, 3, 1, 2),
        "bd": np.stack([a["w_r"], a["w_i"]], 1).reshape(DEPTH, 2, MT, 2, HD, HD).transpose(0, 3, 1, 4, 2, 5),
        "sconv": feature_tiles(a["state_conv"]).transpose(1, 0, 4, 3, 2).reshape(DEPTH, P, -1),
        "sh0": feature_tiles(a["state_h"]).transpose(1, 0, 3, 2).reshape(DEPTH, P, -1),
    }
    outs = {"y": (P, XT, TOK), "st": (P, DEPTH * MT * NS), "v": (DEPTH, NSAMP, WA)}

    nc = bacc.Bacc("TRN2", target_bir_lowering=False, num_devices=1)
    args = []
    for name in arrays:
        args.append(nc.dram_tensor(name + "_dram", arrays[name].shape, F32, kind="ExternalInput").ap())
    for name, shape in outs.items():
        args.append(nc.dram_tensor(name + "_out", shape, F32, kind="ExternalOutput").ap())
    trunk(nc, *args)
    given = {name + "_dram": np.ascontiguousarray(v) for name, v in arrays.items()}
    r = run_bass_kernel_spmd(nc, [given], core_ids=[0]).results[0]

    y = r["y_out"].transpose(1, 0, 2).reshape(DM, TOK).T
    v = r["v_out"]
    st = r["st_out"].reshape(P, DEPTH, MT, NS).transpose(1, 3, 2, 0).reshape(DEPTH, NS, WB)
    c = np.ascontiguousarray
    return (c(y[:SEQ][None]), c(y[SEQ:][:, None]), c(st[:, S_H][:, None]), c(st[:, S_C:S_C + 3][:, None]),
            c(st[:, S_HS:S_HS + NSAMP]),
            c(st[:, S_CS:].reshape(DEPTH, 3, NSAMP, WB).transpose(0, 2, 1, 3)), c(v[:, :, None]))
```
